# Optimizing a Trainium2 kernel written in Bass

```python
import jax, jax.numpy as jnp
from jax import lax
import numpy as np

D_MODEL = 1024
BATCH = 1
SEQ = 128
DEPTH = 2
DEC_BATCH = 1
DEC_SEQ = 512
PAST_LEN = 128

GRID_W = 64
N_MIXERS = 4
DEEPNORM_ALPHA = (2.0 * DEPTH) ** 0.25
DEEPNORM_BETA = (8.0 * DEPTH) ** -0.25
ADA_CHUNKS = 6
NORM_EPS = 1e-5

M_HEADS = 4
M_DK = 128
M_DV = 256
M_CHUNK = 64
M_FGATE_BIAS = 3.0
G_HEADS = 4
G_DK = 128
G_DV = 256
G_GATE_RANK = 16
G_GATE_NORM = 16.0
G_CHUNK = 32
NA_HEADS = 16
NA_HD = 64
NA_ROWS = 8
NA_COLS = 16
NA_BAND = 2 * NA_COLS
NA_NCB = GRID_W // NA_COLS
MLA_HEADS = 16
MLA_Q_LORA = 512
MLA_KV_LORA = 256
MLA_NOPE = 64
MLA_ROPE = 32
MLA_VD = 64
ROPE_BASE = 10000.0
Q_BLOCK = 128
PEER_HEADS = 8
PEER_NKEYS = 128
PEER_EXPERTS = PEER_NKEYS * PEER_NKEYS
PEER_KDIM = 256
PEER_HALF = PEER_KDIM // 2
PEER_TOPK = 16
PEER_TBLOCK = 128

kernel_name = 'hybrid_diffusion_trunk_step'

def _f32(a):
    return a.astype(jnp.float32)

def layer_norm(x, g, b):
    xf = _f32(x)
    mu = jnp.mean(xf, -1, keepdims=True)
    var = jnp.mean(jnp.square(xf - mu), -1, keepdims=True)
    return ((xf - mu) * lax.rsqrt(var + NORM_EPS) * _f32(g) + _f32(b)).astype(x.dtype)

def rms_norm(x, g):
    xf = _f32(x)
    return (xf * lax.rsqrt(jnp.mean(jnp.square(xf), -1, keepdims=True) + NORM_EPS) * _f32(g)).astype(x.dtype)

def adaln(cvec, w, b):
    m = jax.nn.silu(cvec) @ w + b
    return jnp.split(m[:, None, :], ADA_CHUNKS, axis=-1)

def modulate(x, shift, scale):
    return x * (1 + scale) + shift

def _chunks(a, L):
    Bn, T = a.shape[0], a.shape[1]
    return jnp.swapaxes(a.reshape(Bn, T // L, L, *a.shape[2:]), 0, 1)

def _unchunks(a):
    a = jnp.swapaxes(a, 0, 1)
    return a.reshape(a.shape[0], a.shape[1] * a.shape[2], *a.shape[3:])

def _rev(a):
    return jnp.flip(a, axis=1)

def axial_rope(x):
    T, R = x.shape[1], x.shape[-1]
    ra = R // 2
    t = jnp.arange(T)
    inv = 1.0 / (ROPE_BASE ** (jnp.arange(0, ra, 2, dtype=jnp.float32) / ra))
    def rot(xa, pos):
        ang = pos.astype(jnp.float32)[:, None] * inv[None, :]
        cos = jnp.cos(ang)[None, :, None, :]
        sin = jnp.sin(ang)[None, :, None, :]
        x1, x2 = xa[..., :ra // 2], xa[..., ra // 2:]
        return jnp.concatenate([x1 * cos - x2 * sin, x1 * sin + x2 * cos], -1)
    xf = _f32(x)
    out = jnp.concatenate([rot(xf[..., :ra], t // GRID_W), rot(xf[..., ra:], t % GRID_W)], -1)
    return out.astype(x.dtype)

def blocked_attention(q, k, v):
    Bn, Lq, H, dq = q.shape
    scale = dq ** -0.5
    qb = jnp.swapaxes(q.reshape(Bn, Lq // Q_BLOCK, Q_BLOCK, H, dq), 0, 1)
    def one(qi):
        s = _f32(jnp.einsum('bqhd,bkhd->bhqk', qi, k)) * scale
        p = jax.nn.softmax(s, axis=-1).astype(v.dtype)
        return jnp.einsum('bhqk,bkhd->bqhd', p, v)
    return _unchunks(lax.map(one, qb))

def mlstm_scan(q, k, v, logi, logf, C0, n0, m0):
    L = M_CHUNK
    tri = jnp.tril(jnp.ones((L, L), dtype=bool))
    xs = tuple(_chunks(_f32(a), L) for a in (q, k, v, logi, logf))
    def step(carry, inp):
        C, n, m = carry
        qc, kc, vc, li, lf = inp
        b = jnp.swapaxes(jnp.cumsum(lf, axis=1), 1, 2)
        li = jnp.swapaxes(li, 1, 2)
        dmat = jnp.where(tri, b[..., :, None] - b[..., None, :] + li[..., None, :], -jnp.inf)
        inter = b + m[..., None]
        mt = jnp.maximum(inter, jnp.max(dmat, axis=-1))
        s = jnp.einsum('blhd,bshd->bhls', qc, kc) * jnp.exp(dmat - mt[..., None])
        ei = jnp.exp(inter - mt)
        num = jnp.einsum('bhls,bshv->bhlv', s, vc) + ei[..., None] * jnp.einsum('blhd,bhdv->bhlv', qc, C)
        den = jnp.sum(s, -1) + ei * jnp.einsum('blhd,bhd->bhl', qc, n)
        h = num / jnp.maximum(jnp.abs(den), jnp.exp(-mt))[..., None]
        bl = b[..., -1]
        g = bl[..., None] - b + li
        m_new = jnp.maximum(bl + m, jnp.max(g, -1))
        wk = jnp.exp(g - m_new[..., None])
        dec = jnp.exp(bl + m - m_new)
        C_new = dec[..., None, None] * C + jnp.einsum('bhs,bshd,bshv->bhdv', wk, kc, vc)
        n_new = dec[..., None] * n + jnp.einsum('bhs,bshd->bhd', wk, kc)
        return (C_new, n_new, m_new), jnp.swapaxes(h, 1, 2)
    (C, n, m), hs = lax.scan(step, (_f32(C0), _f32(n0), _f32(m0)), xs)
    return _unchunks(hs), C, n, m

def mlstm_mixer(h, C0, n0, m0, w_in, b_gate, norm_w, w_out):
    Bn, T, _ = h.shape
    hk, hv = M_HEADS * M_DK, M_HEADS * M_DV
    p = h @ w_in
    q = p[..., :hk].reshape(Bn, T, M_HEADS, M_DK)
    k = p[..., hk:2 * hk].reshape(Bn, T, M_HEADS, M_DK) * (M_DK ** -0.5)
    v = p[..., 2 * hk:2 * hk + hv].reshape(Bn, T, M_HEADS, M_DV)
    o = p[..., 2 * hk + hv:2 * hk + 2 * hv]
    gates = (_f32(p[..., 2 * hk + 2 * hv:]) + _f32(b_gate)).reshape(Bn, T, 4, M_HEADS)
    hf, Cf, nf, mf = mlstm_scan(q, k, v, gates[:, :, 0], jax.nn.log_sigmoid(gates[:, :, 1]),
                                C0[:, 0], n0[:, 0], m0[:, 0])
    hb, Cb, nb, mb = mlstm_scan(_rev(q), _rev(k), _rev(v), _rev(gates[:, :, 2]),
                                _rev(jax.nn.log_sigmoid(gates[:, :, 3])), C0[:, 1], n0[:, 1], m0[:, 1])
    hs = hf + _rev(hb)
    mu = jnp.mean(hs, -1, keepdims=True)
    var = jnp.mean(jnp.square(hs - mu), -1, keepdims=True)
    hn = (hs - mu) * lax.rsqrt(var + NORM_EPS) * _f32(norm_w).reshape(M_HEADS, M_DV)
    y = (jax.nn.sigmoid(_f32(o)) * hn.reshape(Bn, T, hv)).astype(h.dtype) @ w_out
    return y, jnp.stack([Cf, Cb], 1), jnp.stack([nf, nb], 1), jnp.stack([mf, mb], 1)

def gla_scan(q, k, v, loga, S0):
    L = G_CHUNK
    tri = jnp.tril(jnp.ones((L, L), dtype=bool))
    xs = tuple(_chunks(_f32(a), L) for a in (q, k, v, loga))
    def step(S, inp):
        qc, kc, vc, la = inp
        bc = jnp.cumsum(la, axis=1)
        qd = qc * jnp.exp(bc)
        kd = kc * jnp.exp(-bc)
        a = jnp.where(tri, jnp.einsum('blhd,bshd->bhls', qd, kd), 0.0)
        o = jnp.einsum('bhls,bshv->blhv', a, vc) + jnp.einsum('blhd,bhdv->blhv', qd, S)
        bl = bc[:, -1]
        kl = kc * jnp.exp(bl[:, None] - bc)
        S_new = jnp.exp(bl)[..., None] * S + jnp.einsum('blhd,blhv->bhdv', kl, vc)
        return S_new, o
    S, os_ = lax.scan(step, _f32(S0), xs)
    return _unchunks(os_), S

def gla_mixer(h, S0, w_in, w_gate2, b_gate2, norm_w, w_out):
    Bn, T, _ = h.shape
    hk, hv = G_HEADS * G_DK, G_HEADS * G_DV
    p = h @ w_in
    q = p[..., :hk].reshape(Bn, T, G_HEADS, G_DK) * (G_DK ** -0.5)
    k = p[..., hk:2 * hk].reshape(Bn, T, G_HEADS, G_DK)
    v = p[..., 2 * hk:2 * hk + hv].reshape(Bn, T, G_HEADS, G_DV)
    g = p[..., 2 * hk + hv:2 * hk + 2 * hv]
    gr = p[..., 2 * hk + 2 * hv:].reshape(Bn, T, 2, G_GATE_RANK)
    loga = jax.nn.log_sigmoid(_f32(jnp.einsum('btzr,zrk->btzk', gr, w_gate2)) + _f32(b_gate2)) / G_GATE_NORM
    loga = loga.reshape(Bn, T, 2, G_HEADS, G_DK)
    of, Sf = gla_scan(q, k, v, loga[:, :, 0], S0[:, 0])
    ob, Sb = gla_scan(_rev(q), _rev(k), _rev(v), _rev(loga[:, :, 1]), S0[:, 1])
    o = of + _rev(ob)
    on = o * lax.rsqrt(jnp.mean(jnp.square(o), -1, keepdims=True) + NORM_EPS) * _f32(norm_w)
    y = (jax.nn.silu(_f32(g)) * on.reshape(Bn, T, hv)).astype(h.dtype) @ w_out
    return y, jnp.stack([Sf, Sb], 1)

def na_project(h, w_in):
    Bn, T, _ = h.shape
    qkv = (h @ w_in).reshape(Bn, T, 3, NA_HEADS, NA_HD)
    return qkv[:, :, 0], qkv[:, :, 1], qkv[:, :, 2]

def na_latent(q, k, v, k_ctx, v_ctx, rpb):
    Bn, T, H, Dh = q.shape
    rows = T // GRID_W
    wr = min(NA_ROWS, rows)
    scale = Dh ** -0.5
    col_q = np.arange(GRID_W).reshape(NA_NCB, NA_COLS)
    band = np.clip(np.arange(NA_NCB) * NA_COLS - NA_COLS // 2, 0, GRID_W - NA_BAND)[:, None] + np.arange(NA_BAND)[None, :]
    cs = np.clip(col_q - NA_COLS // 2, 0, GRID_W - NA_COLS)
    col_ok = (band[:, None, :] >= cs[:, :, None]) & (band[:, None, :] < cs[:, :, None] + NA_COLS)
    dc = np.clip(band[:, None, :] - col_q[:, :, None], -(NA_COLS - 1), NA_COLS - 1) + (NA_COLS - 1)
    rpb_c = _f32(rpb)[:, :, dc]
    qg = q.reshape(Bn, rows, GRID_W, H, Dh)
    kg = k.reshape(Bn, rows, GRID_W, H, Dh)
    vg = v.reshape(Bn, rows, GRID_W, H, Dh)
    nloc = wr * NA_BAND
    def one_row(args):
        qr, r = args
        start = jnp.clip(r - wr // 2, 0, rows - wr)
        kb = lax.dynamic_slice_in_dim(kg, start, wr, axis=1)[:, :, band]
        vb = lax.dynamic_slice_in_dim(vg, start, wr, axis=1)[:, :, band]
        dr = start + jnp.arange(wr) - r + (NA_ROWS - 1)
        bias = jnp.transpose(rpb_c[:, dr], (0, 2, 3, 1, 4))
        qc = qr.reshape(Bn, NA_NCB, NA_COLS, H, Dh)
        s_loc = _f32(jnp.einsum('bcqhd,bacwhd->bhcqaw', qc, kb)) * scale + bias[None]
        s_loc = jnp.where(col_ok[:, :, None, :], s_loc, -jnp.inf).reshape(Bn, H, NA_NCB, NA_COLS, nloc)
        s_ctx = _f32(jnp.einsum('bcqhd,bkhd->bhcqk', qc, k_ctx)) * scale
        p = jax.nn.softmax(jnp.concatenate([s_loc, s_ctx], -1), axis=-1).astype(v.dtype)
        p_loc = p[..., :nloc].reshape(Bn, H, NA_NCB, NA_COLS, wr, NA_BAND)
        o = jnp.einsum('bhcqaw,bacwhd->bcqhd', p_loc, vb) + jnp.einsum('bhcqk,bkhd->bcqhd', p[..., nloc:], v_ctx)
        return o.reshape(Bn, GRID_W, H, Dh)
    o = lax.map(one_row, (jnp.swapaxes(qg, 0, 1), jnp.arange(rows)))
    return jnp.swapaxes(o, 0, 1).reshape(Bn, T, H, Dh)

def mla_project(h, w_in, q_norm, w_qup, kv_norm):
    Bn, T, _ = h.shape
    p = h @ w_in
    cq = p[..., :MLA_Q_LORA]
    ckv = p[..., MLA_Q_LORA:MLA_Q_LORA + MLA_KV_LORA]
    kpe = p[..., MLA_Q_LORA + MLA_KV_LORA:]
    q = (rms_norm(cq, q_norm) @ w_qup).reshape(Bn, T, MLA_HEADS, MLA_NOPE + MLA_ROPE)
    return q, rms_norm(ckv, kv_norm), kpe

def mla_keys(ckv, kpe, w_kvup):
    Bn, L, _ = ckv.shape
    kv = (ckv @ w_kvup).reshape(Bn, L, MLA_HEADS, MLA_NOPE + MLA_VD)
    k = jnp.concatenate([kv[..., :MLA_NOPE],
                         jnp.broadcast_to(kpe[:, :, None, :], (Bn, L, MLA_HEADS, MLA_ROPE)).astype(kv.dtype)], -1)
    return k, kv[..., MLA_NOPE:]

def peer_ffn(x, w_q, subkeys, u_tab, v_tab):
    Bn, T, D = x.shape
    xb = x.reshape(Bn * T // PEER_TBLOCK, PEER_TBLOCK, D)
    def block(xt):
        qh = _f32(xt @ w_q).reshape(PEER_TBLOCK, PEER_HEADS, 2, PEER_HALF)
        s = jnp.einsum('thpd,hpnd->thpn', qh, _f32(subkeys))
        v_top, i_top = lax.top_k(s, PEER_TOPK)
        cand = (v_top[:, :, 0, :, None] + v_top[:, :, 1, None, :]).reshape(PEER_TBLOCK, PEER_HEADS, PEER_TOPK * PEER_TOPK)
        cidx = (i_top[:, :, 0, :, None] * PEER_NKEYS + i_top[:, :, 1, None, :]).reshape(PEER_TBLOCK, PEER_HEADS, PEER_TOPK * PEER_TOPK)
        sc, pos = lax.top_k(cand, PEER_TOPK)
        eidx = jnp.take_along_axis(cidx, pos, axis=-1).reshape(PEER_TBLOCK, PEER_HEADS * PEER_TOPK)
        gate = jax.nn.softmax(sc, axis=-1).reshape(PEER_TBLOCK, PEER_HEADS * PEER_TOPK)
        act = jax.nn.gelu(_f32(jnp.einsum('td,ted->te', xt, u_tab[eidx])))
        return jnp.einsum('te,ted->td', (gate * act).astype(xt.dtype), v_tab[eidx])
    return lax.map(block, xb).reshape(Bn, T, D)

def setup_inputs(seed: int = 0) -> dict:
    key = jax.random.key(seed)
    keys = jax.random.split(key, 64)
    counter = [0]
    def nrm(shape, scale):
        kk = keys[counter[0]]
        counter[0] += 1
        return jax.random.normal(kk, shape, jnp.float32) * scale
    D = D_MODEL
    fan = D ** -0.5
    inp = {}
    inp['x_prompt'] = nrm((BATCH, SEQ, D), 1.0)
    inp['x_sample'] = nrm((DEC_BATCH, DEC_SEQ, D), 1.0)
    inp['c'] = nrm((DEC_BATCH, D), 1.0)
    inp['c_ctx'] = nrm((D,), 1.0)
    inp['state_mlstm_C'] = nrm((DEC_BATCH, 2, M_HEADS, M_DK, M_DV), 0.1)
    inp['state_mlstm_n'] = nrm((DEC_BATCH, 2, M_HEADS, M_DK), 0.1)
    inp['state_mlstm_m'] = nrm((DEC_BATCH, 2, M_HEADS), 1.0)
    inp['state_gla_S'] = nrm((DEC_BATCH, 2, G_HEADS, G_DK, G_DV), 0.1)
    inp['cache_na_k'] = nrm((DEC_BATCH, PAST_LEN, NA_HEADS, NA_HD), 1.0)
    inp['cache_na_v'] = nrm((DEC_BATCH, PAST_LEN, NA_HEADS, NA_HD), 1.0)
    inp['cache_mla_ckv'] = nrm((DEC_BATCH, PAST_LEN, MLA_KV_LORA), 1.0)
    inp['cache_mla_kpe'] = nrm((DEC_BATCH, PAST_LEN, MLA_ROPE), 1.0)
    inp['ada_w'] = nrm((DEPTH, D, ADA_CHUNKS * D), fan)
    inp['ada_b'] = nrm((DEPTH, ADA_CHUNKS * D), 0.1)
    inp['ln_mix_g'] = 1.0 + nrm((DEPTH, D), 0.05)
    inp['ln_mix_b'] = nrm((DEPTH, D), 0.05)
    inp['ln_ffn_g'] = 1.0 + nrm((DEPTH, D), 0.05)
    inp['ln_ffn_b'] = nrm((DEPTH, D), 0.05)
    m_cols = 2 * M_HEADS * M_DK + 2 * M_HEADS * M_DV + 4 * M_HEADS
    inp['mlstm_w_in'] = nrm((D, m_cols), fan)
    inp['mlstm_b_gate'] = nrm((4 * M_HEADS,), 0.1) + jnp.repeat(jnp.array([0.0, M_FGATE_BIAS, 0.0, M_FGATE_BIAS], jnp.float32), M_HEADS)
    inp['mlstm_norm_w'] = 1.0 + nrm((M_HEADS * M_DV,), 0.05)
    inp['mlstm_w_out'] = nrm((M_HEADS * M_DV, D), (M_HEADS * M_DV) ** -0.5 * DEEPNORM_BETA)
    g_cols = 2 * G_HEADS * G_DK + 2 * G_HEADS * G_DV + 2 * G_GATE_RANK
    inp['gla_w_in'] = nrm((D, g_cols), fan)
    inp['gla_w_gate2'] = nrm((2, G_GATE_RANK, G_HEADS * G_DK), G_GATE_RANK ** -0.5)
    inp['gla_b_gate2'] = nrm((2, G_HEADS * G_DK), 0.1)
    inp['gla_norm_w'] = 1.0 + nrm((G_DV,), 0.05)
    inp['gla_w_out'] = nrm((G_HEADS * G_DV, D), (G_HEADS * G_DV) ** -0.5 * DEEPNORM_BETA)
    inp['na_w_in'] = nrm((D, 3 * NA_HEADS * NA_HD), fan)
    inp['na_rpb'] = nrm((NA_HEADS, 2 * NA_ROWS - 1, 2 * NA_COLS - 1), 0.5)
    inp['na_w_out'] = nrm((NA_HEADS * NA_HD, D), (NA_HEADS * NA_HD) ** -0.5 * DEEPNORM_BETA)
    inp['mla_w_in'] = nrm((D, MLA_Q_LORA + MLA_KV_LORA + MLA_ROPE), fan)
    inp['mla_q_norm'] = 1.0 + nrm((MLA_Q_LORA,), 0.05)
    inp['mla_w_qup'] = nrm((MLA_Q_LORA, MLA_HEADS * (MLA_NOPE + MLA_ROPE)), MLA_Q_LORA ** -0.5)
    inp['mla_kv_norm'] = 1.0 + nrm((MLA_KV_LORA,), 0.05)
    inp['mla_w_kvup'] = nrm((MLA_KV_LORA, MLA_HEADS * (MLA_NOPE + MLA_VD)), MLA_KV_LORA ** -0.5)
    inp['mla_w_out'] = nrm((MLA_HEADS * MLA_VD, D), (MLA_HEADS * MLA_VD) ** -0.5 * DEEPNORM_BETA)
    inp['peer_w_q'] = nrm((DEPTH, D, PEER_HEADS * PEER_KDIM), fan)
    inp['peer_subkeys'] = nrm((DEPTH, PEER_HEADS, 2, PEER_NKEYS, PEER_HALF), PEER_HALF ** -0.5)
    inp['peer_u'] = nrm((DEPTH, PEER_EXPERTS, D), fan)
    inp['peer_v'] = nrm((DEPTH, PEER_EXPERTS, D), DEEPNORM_BETA)
    return inp

def reference(x_prompt, x_sample, c, c_ctx, state_mlstm_C, state_mlstm_n, state_mlstm_m, state_gla_S,
              cache_na_k, cache_na_v, cache_mla_ckv, cache_mla_kpe,
              ada_w, ada_b, ln_mix_g, ln_mix_b, ln_ffn_g, ln_ffn_b,
              mlstm_w_in, mlstm_b_gate, mlstm_norm_w, mlstm_w_out,
              gla_w_in, gla_w_gate2, gla_b_gate2, gla_norm_w, gla_w_out,
              na_w_in, na_rpb, na_w_out,
              mla_w_in, mla_q_norm, mla_w_qup, mla_kv_norm, mla_w_kvup, mla_w_out,
              peer_w_q, peer_subkeys, peer_u, peer_v):
    xp, xs = x_prompt, x_sample
    Bp, Lp = xp.shape[0], xp.shape[1]
    Bs, Ts = xs.shape[0], xs.shape[1]
    new_mlstm_C = new_mlstm_n = new_mlstm_m = new_gla_S = None
    new_na_k = new_na_v = new_mla_ckv = new_mla_kpe = None
    for l in range(DEPTH):
        kind = l % N_MIXERS
        mp = adaln(c_ctx[None, :], ada_w[l], ada_b[l])
        ms = adaln(c, ada_w[l], ada_b[l])
        hp = modulate(xp, mp[0], mp[1])
        hs = modulate(xs, ms[0], ms[1])
        if kind == 0:
            zC = jnp.zeros((Bp, 2, M_HEADS, M_DK, M_DV), jnp.float32)
            zn = jnp.zeros((Bp, 2, M_HEADS, M_DK), jnp.float32)
            zm = jnp.zeros((Bp, 2, M_HEADS), jnp.float32)
            yp, new_mlstm_C, new_mlstm_n, new_mlstm_m = mlstm_mixer(hp, zC, zn, zm, mlstm_w_in, mlstm_b_gate, mlstm_norm_w, mlstm_w_out)
            ys, _, _, _ = mlstm_mixer(hs, state_mlstm_C, state_mlstm_n, state_mlstm_m, mlstm_w_in, mlstm_b_gate, mlstm_norm_w, mlstm_w_out)
        elif kind == 1:
            zS = jnp.zeros((Bp, 2, G_HEADS, G_DK, G_DV), jnp.float32)
            yp, new_gla_S = gla_mixer(hp, zS, gla_w_in, gla_w_gate2, gla_b_gate2, gla_norm_w, gla_w_out)
            ys, _ = gla_mixer(hs, state_gla_S, gla_w_in, gla_w_gate2, gla_b_gate2, gla_norm_w, gla_w_out)
        elif kind == 2:
            qp, kp, vp = na_project(hp, na_w_in)
            yp = blocked_attention(qp, kp, vp).reshape(Bp, Lp, NA_HEADS * NA_HD) @ na_w_out
            new_na_k, new_na_v = kp, vp
            ql, kl, vl = na_project(hs, na_w_in)
            ys = na_latent(ql, kl, vl, cache_na_k, cache_na_v, na_rpb).reshape(Bs, Ts, NA_HEADS * NA_HD) @ na_w_out
        else:
            qp, ckvp, kpep = mla_project(hp, mla_w_in, mla_q_norm, mla_w_qup, mla_kv_norm)
            kp, vp = mla_keys(ckvp, kpep, mla_w_kvup)
            yp = blocked_attention(qp, kp, vp).reshape(Bp, Lp, MLA_HEADS * MLA_VD) @ mla_w_out
            new_mla_ckv, new_mla_kpe = ckvp, kpep
            ql, ckvl, kpel = mla_project(hs, mla_w_in, mla_q_norm, mla_w_qup, mla_kv_norm)
            ql = jnp.concatenate([ql[..., :MLA_NOPE], axial_rope(ql[..., MLA_NOPE:])], -1)
            kpel = axial_rope(kpel[:, :, None, :])[:, :, 0]
            kl, vl = mla_keys(ckvl, kpel, mla_w_kvup)
            kc, vc = mla_keys(cache_mla_ckv, cache_mla_kpe, mla_w_kvup)
            ys = blocked_attention(ql, jnp.concatenate([kl, kc], 1), jnp.concatenate([vl, vc], 1))
            ys = ys.reshape(Bs, Ts, MLA_HEADS * MLA_VD) @ mla_w_out
        xp = layer_norm(DEEPNORM_ALPHA * xp + mp[2] * yp, ln_mix_g[l], ln_mix_b[l])
        xs = layer_norm(DEEPNORM_ALPHA * xs + ms[2] * ys, ln_mix_g[l], ln_mix_b[l])
        fp = peer_ffn(modulate(xp, mp[3], mp[4]), peer_w_q[l], peer_subkeys[l], peer_u[l], peer_v[l])
        fs = peer_ffn(modulate(xs, ms[3], ms[4]), peer_w_q[l], peer_subkeys[l], peer_u[l], peer_v[l])
        xp = layer_norm(DEEPNORM_ALPHA * xp + mp[5] * fp, ln_ffn_g[l], ln_ffn_b[l])
        xs = layer_norm(DEEPNORM_ALPHA * xs + ms[5] * fs, ln_ffn_g[l], ln_ffn_b[l])
    return (xp, xs, new_mlstm_C, new_mlstm_n, new_mlstm_m, new_gla_S, new_na_k, new_na_v, new_mla_ckv, new_mla_kpe)


_drawn_inputs = setup_inputs


def setup_inputs(seed=0):
    import zlib

    import numpy as np

    out = dict(_drawn_inputs(seed))
    spreads = {}
    factors = {'state_mlstm_C': 4.13,
     'state_mlstm_n': 6.544,
     'state_mlstm_m': 4.998,
     'state_gla_S': 32.343,
     'mlstm_norm_w': 2.819,
     'gla_norm_w': 3.555}
    for name, (base, spread) in spreads.items():
        noise = np.random.default_rng([zlib.crc32(name.encode()), seed]).standard_normal(out[name].shape)
        drawn = base * np.exp(spread * noise) if base else spread * noise
        out[name] = __import__('jax').numpy.asarray(drawn.astype(out[name].dtype))
    for name, factor in factors.items():
        out[name] = (out[name] * factor).astype(out[name].dtype)
    return out
```

```python
from contextlib import ExitStack

import numpy as np

import concourse.bass as bass
from concourse import mybir

F32 = mybir.dt.float32
U32 = mybir.dt.uint32
ALU = mybir.AluOpType
ACT = mybir.ActivationFunctionType
AX = mybir.AxisListType

P = 128
D = 1024
KD = D // P
HALF = 512
SEQ, DEC_SEQ = 128, 512
NT = (SEQ + DEC_SEQ) // P
LAYERS = 2
CHUNKS = 6
ALPHA = (2.0 * LAYERS) ** 0.25
EPS = 1e-5
NH, DK, DV = 4, 128, 256
HV = NH * DV
NP_ = 2 * NH * DK + 2 * HV
NG = NP_ // HALF
NEG = -1.0e30
EH, TOPK, NKEYS = 8, 16, 128
GATE_NORM = 16.0
RANK = 16
TANH_SCALE = float(np.sqrt(2.0 / np.pi))
NB, BL = 4, 32
RING = 8


def constants():
    i, j = np.arange(P)[:, None], np.arange(P)[None, :]
    parts = {
        "ident": i == j,
        "le": i <= j, "ge": i >= j,
        "le16": (i <= j) / GATE_NORM, "ge16": (i >= j) / GATE_NORM,
        "gt16": (i > j) / GATE_NORM, "lt16": (i < j) / GATE_NORM,
        "neg_f": np.where(j <= i, 0.0, NEG), "neg_b": np.where(j >= i, 0.0, NEG),
        "last": np.broadcast_to(i == P - 1, (P, P)), "first": np.broadcast_to(i == 0, (P, P)),
        "sel": i == np.arange(NT * NH)[None, :],
        "iota": np.broadcast_to(np.arange(TOPK)[None, :], (P, TOPK)),
        "ones": np.ones((P, P)),
    }
    at, where = 0, {}
    for name, a in parts.items():
        where[name] = (at, a.shape[1])
        at += a.shape[1]
    return np.concatenate([np.asarray(a, np.float32) for a in parts.values()], 1), where


class Mem:
    pass


def allocate(nc, ctx, const_cols):
    m = Mem()

    def sb(name, shape, dt=F32):
        return ctx.enter_context(nc.sbuf_tensor(name, shape, dt))

    m.X = sb("X", [P, NT, D])
    m.mod = sb("mod", [P, 3, 2, D])
    m.lnw = sb("lnw", [P, 2, D])
    m.cst = sb("cst", [P, const_cols])
    m.big = sb("big", [P, 2 * RING * D])
    m.wrk = sb("wrk", [P, 14336])
    m.W = m.wrk[:, 0:8192].rearrange("p (s k n) -> p s k n", s=2, k=KD)
    m.hT = m.wrk[:, 8192:13312].rearrange("p (t k n) -> p t k n", t=NT, k=KD)
    m.H = m.wrk[:, 8192:13312].rearrange("p (t n) -> p t n", t=NT)
    m.y = sb("y", [P, D])
    m.yT = sb("yT", [P, KD, P])
    m.proj = m.big[:, 0:NT * NP_].rearrange("p (t n) -> p t n", t=NT)
    m.gates = sb("gates", [P, NT, 32])
    m.stat = sb("stat", [P, 64])
    m.scr = sb("scr", [P, 512])
    m.qk = sb("qk", [P, 4 * HALF])
    m.hot = sb("hot", [P, 2 * TOPK * TOPK])
    m.qhT = sb("qhT", [P, 2, 2 * P])
    m.route_gate = sb("route_gate", [P, NT * EH * TOPK])
    m.ps = ctx.enter_context(nc.psum_tensor("ps", [P, 8, HALF], F32))
    m.sb = sb
    return m


class Stage:

    def __init__(self, nc, name):
        self.nc, self.name, self.sems, self.ctx = nc, name, [], ExitStack()

    def sem(self, name):
        self.sems.append(self.nc.alloc_semaphore(f"{self.name}_{name}"))
        return self.sems[-1]

    def block(self):
        return self.ctx.enter_context(self.nc.Block())

    def __enter__(self):
        return self

    def __exit__(self, *failed):
        self.ctx.__exit__(*failed)
        if failed[0] is None:
            self.nc.clear_and_free_semaphores(self.sems)
            self.nc.all_engine_barrier()


def load_constants(nc, m, a):
    with Stage(nc, "load") as st:
        loaded = st.sem("loaded")
        block = st.block()

        @block.sync
        def _(sp):
            sp.dma_start(m.cst[:], a["cst"]).then_inc(loaded, 16)
            sp.dma_start(m.X[:, 0, :], a["x_prompt"][0]).then_inc(loaded, 16)
            sp.dma_start(m.X[:, 1:NT, :], a["x_sample"][0].rearrange("(t p) d -> p t d", p=P)).then_inc(loaded, 16)
            sp.wait_ge(loaded, 48)


def modulation_rows(nc, m, a, layer):
    NGRP = CHUNKS * D // HALF
    w = a["ada_w"][layer].rearrange("(k p) n -> p k n", p=P)
    with Stage(nc, f"mod{layer}") as st:
        w_full = [st.sem("w_full0"), st.sem("w_full1")]
        ps_full, row_done, c_loaded, c_step, stored = (
            st.sem(n) for n in ("ps_full", "row_done", "c_loaded", "c_step", "stored"))
        rows = m.big[0:2, 0:CHUNKS * D]
        bias = m.big[0:2, CHUNKS * D:2 * CHUNKS * D]
        cv = m.y[:, 0:2 * KD]
        ex = m.y[:, 2 * KD:4 * KD]
        cs = m.y[:, 4 * KD:6 * KD]
        block = st.block()

        @block.sync
        def _(sp):
            sp.dma_start(cv, a["c2"]).then_inc(c_loaded, 16)
            for c in range(2):
                sp.dma_start(bias[c:c + 1, :], a["ada_b"][layer:layer + 1, :]).then_inc(c_loaded, 16)

            def load(it, first):
                for s in range(2):
                    g = it * 2 + s
                    if not first:
                        sp.wait_ge(ps_full, g - 1)
                    sp.dma_start(m.W[:, s], w[:, :, bass.ds(g * HALF, HALF)]).then_inc(w_full[s], 16)

            load(0, True)
            with sp.Fori(1, NGRP // 2) as it:
                load(it, False)
            sp.wait_ge(row_done, NGRP + 2)
            sp.dma_start(a["rows"][layer], rows).then_inc(stored, 16)
            sp.wait_ge(stored, 16)

        @block.tensor
        def _(pe):
            pe.wait_ge(c_step, 4)

            def products(it, first):
                for s in range(2):
                    g = it * 2 + s
                    pe.wait_ge(w_full[s], it * 16 + 16)
                    if not first:
                        pe.wait_ge(row_done, g - 1)
                    for k in range(KD):
                        mm = pe.matmul(m.ps[0:2, s, :], cs[:, 2 * k:2 * k + 2], m.W[:, s, k, :],
                                       start=k == 0, stop=k == KD - 1)
                    mm.then_inc(ps_full, 1)

            products(0, True)
            with pe.Fori(1, NGRP // 2) as it:
                products(it, False)

        @block.scalar
        def _(act):
            act.wait_ge(c_loaded, 48)
            act.activation(ex, cv, ACT.Exp, scale=-1.0).then_inc(c_step, 1)

        @block.vector
        def _(dve):
            dve.wait_ge(c_step, 1)
            dve.tensor_scalar(ex, ex, 1.0, None, ALU.add).then_inc(c_step, 1)
            dve.wait_ge(c_step, 2)
            dve.reciprocal(ex, ex).then_inc(c_step, 1)
            dve.wait_ge(c_step, 3)
            dve.tensor_tensor(cs, ex, cv, ALU.mult).then_inc(c_step, 1)
            with dve.Fori(0, NGRP // 2) as it:
                for s in range(2):
                    g = it * 2 + s
                    dve.wait_ge(ps_full, g + 1)
                    dve.tensor_tensor(rows[:, bass.ds(g * HALF, HALF)], m.ps[0:2, s, :],
                                      bias[:, bass.ds(g * HALF, HALF)], ALU.add).then_inc(row_done, 1)
            dve.wait_ge(row_done, NGRP)
            for n in (1, 4):
                row = rows[:, n * D:(n + 1) * D]
                dve.tensor_scalar(row, row, 1.0, None, ALU.add).then_inc(row_done, 1)


def load_modulation(nc, m, a, layer, first, which, ln):
    with Stage(nc, f"rows{layer}{ln}{first}") as st:
        loaded = st.sem("loaded")
        block = st.block()

        @block.sync
        def _(sp):
            n_loads = 0
            for n in which:
                for c in range(2):
                    row = a["rows"][layer, c, (first + n) * D:(first + n + 1) * D]
                    sp.dma_start(m.mod[:, n, c, :], row.partition_broadcast(P)).then_inc(loaded, 16)
                    n_loads += 1
            for n, name in enumerate(("g", "b")):
                row = a[f"ln_{ln}_{name}"][layer]
                sp.dma_start(m.lnw[:, n, :], row.partition_broadcast(P)).then_inc(loaded, 16)
                n_loads += 1
            sp.wait_ge(loaded, 16 * n_loads)


def modulate_transpose(nc, m, a, layer):
    with Stage(nc, f"mt{layer}") as st:
        modulated, transposed, copied = (st.sem(n) for n in ("modulated", "transposed", "copied"))
        block = st.block()

        @block.vector
        def _(dve):
            def tile(t, c, first):
                if not first:
                    dve.wait_ge(transposed, t)
                dve.tensor_tensor(m.y[:], m.X[:, t, :], m.mod[:, 1, c, :], ALU.mult).then_inc(modulated, 1)
                dve.wait_ge(modulated, t * 2 + 1)
                dve.tensor_tensor(m.y[:], m.y[:], m.mod[:, 0, c, :], ALU.add).then_inc(modulated, 1)

            tile(0, 0, True)
            with dve.Fori(1, NT) as t:
                tile(t, 1, False)

        @block.tensor
        def _(pe):
            def tile(t, first):
                if not first:
                    pe.wait_ge(copied, t)
                pe.wait_ge(modulated, t * 2 + 2)
                for k in range(KD):
                    tr = pe.transpose(m.ps[:, k // 4, (k % 4) * P:(k % 4 + 1) * P], m.y[:, k * P:(k + 1) * P], m.ident)
                tr.then_inc(transposed, 1)

            tile(0, True)
            with pe.Fori(1, NT) as t:
                tile(t, False)

        @block.scalar
        def _(act):
            with act.Fori(0, NT) as t:
                act.wait_ge(transposed, t + 1)
                act.copy(m.hT[:, t, :, :].rearrange("p k n -> p (k n)"),
                         m.ps[:, 0:2, :].rearrange("p b n -> p (b n)")).then_inc(copied, 1)


def project(nc, m, a, layer):
    w_in = a[("mlstm_w_in", "gla_w_in")[layer]]
    G = w_in.shape[1] - NP_
    gate = (ACT.Sigmoid, ACT.Silu)[layer]
    w = w_in.rearrange("(k p) n -> p k n", p=P)
    BANKS = 5
    with Stage(nc, f"proj{layer}") as st:
        w_full = [st.sem("w_full0"), st.sem("w_full1")]
        wg_full, ps_full, ps_read = (st.sem(n) for n in ("wg_full", "ps_full", "ps_read"))
        wg = m.y[:, 0:KD * 32].rearrange("p (k g) -> p k g", k=KD)[:, :, 0:G]
        block = st.block()

        @block.sync
        def _(sp):
            sp.dma_start(wg, w[:, :, NP_:NP_ + G]).then_inc(wg_full, 16)

            def load(it, first):
                for s in range(2):
                    if not first:
                        sp.wait_ge(ps_full, (it * 2 + s - 1) * NT + 1)
                    sp.dma_start(m.W[:, s], w[:, :, bass.ds((it * 2 + s) * HALF, HALF)]).then_inc(w_full[s], 16)

            load(0, True)
            with sp.Fori(1, NG // 2) as it:
                load(it, False)

        @block.tensor
        def _(pe):
            pe.wait_ge(wg_full, 16)
            for t in range(NT):
                for k in range(KD):
                    mm = pe.matmul(m.ps[:, 7, t * G:(t + 1) * G], m.hT[:, t, k, :], wg[:, k, :],
                                   start=k == 0, stop=k == KD - 1)
            mm.then_inc(ps_full, 1)

            def products(it, first):
                for s in range(2):
                    pe.wait_ge(w_full[s], it * 16 + 16)
                    for t in range(NT):
                        u = s * NT + t
                        if not first or u >= BANKS:
                            pe.wait_ge(ps_read, it * 2 * NT + u - BANKS + 2)
                        for k in range(KD):
                            mm = pe.matmul(m.ps[:, u % BANKS, :], m.hT[:, t, k, :], m.W[:, s, k, :],
                                           start=k == 0, stop=k == KD - 1)
                        mm.then_inc(ps_full, 1)

            products(0, True)
            with pe.Fori(1, NG // 2) as it:
                products(it, False)

        @block.scalar
        def _(act):
            act.wait_ge(ps_full, 1)
            act.copy(m.gates[:, :, 0:G], m.ps[:, 7, 0:NT * G].rearrange("p (t g) -> p t g", t=NT)).then_inc(ps_read, 1)

            def read(it, func):
                for s in range(2):
                    for t in range(NT):
                        u = s * NT + t
                        act.wait_ge(ps_full, it * 2 * NT + u + 2)
                        act.activation(m.proj[:, t, bass.ds((it * 2 + s) * HALF, HALF)],
                                       m.ps[:, u % BANKS, :], func).then_inc(ps_read, 1)

            with act.Fori(0, NG // 2 - 1) as it:
                read(it, ACT.Copy)
            read(NG // 2 - 1, gate)


def view_constants(m, where):
    view = lambda name: m.cst[:, where[name][0]:where[name][0] + where[name][1]]
    m.ident = view("ident")
    m.le = view("le")
    m.ge = view("ge")
    m.le16 = view("le16")
    m.ge16 = view("ge16")
    m.gt16 = view("gt16")
    m.lt16 = view("lt16")
    m.neg_f = view("neg_f")
    m.neg_b = view("neg_b")
    m.last = view("last")
    m.first = view("first")
    m.sel = view("sel")
    m.iota = view("iota")
    m.ones = view("ones")


class Order:

    def __init__(self, sem, steps):
        self.sem, self.steps = sem, steps.split()

    def at(self, i, step):
        return i * len(self.steps) + self.steps.index(step) + 1


def is_first(i):
    return isinstance(i, int) and i == 0


def tiles_of(engine, i):
    return (0, 0) if isinstance(i, int) else (i, engine.snap(i * -1 + NT))


def mlstm_scan(nc, m, a):
    FW, BW = 0, 1
    base = [m.wrk[:, 0:8192], m.mod[:].rearrange("p a c n -> p (a c n)")]
    at = [0]

    def part(n):
        at[0] += n
        return [b[:, at[0] - n:at[0]] for b in base]

    qk, qT, kT, E, ST, kw, qs, qsT = part(2 * HALF), *(part(HALF) for _ in range(7))
    C = part(NH * DV)
    small = [m.scr[:, 0:64], m.scr[:, 64:128]]
    amax, mu, mprev, blm, den, n_st = ([s[:, 4 * j:4 * j + 4] for s in small] for j in range(6))
    bm = [s[:, 24:32] for s in small]
    last = [s[:, 32:40] for s in small]
    args = [s[:, 40:56] for s in small]
    b_all = [m.scr[:, 128 + 32 * d:128 + 32 * d + NT * NH].rearrange("p (t h) -> p t h", t=NT) for d in range(2)]
    a_all = [m.scr[:, 192 + 32 * d:192 + 32 * d + NT * NH].rearrange("p (t h) -> p t h", t=NT) for d in range(2)]
    lf = [m.scr[:, 256 + 32 * d:256 + 32 * d + NT * NH] for d in range(2)]
    tmp = [m.scr[:, 320 + 32 * d:320 + 32 * d + NT * NH] for d in range(2)]
    bg = m.scr[:, 384:400]
    G = m.gates[:, :, 0:16].rearrange("p t (d k h) -> p d k t h", d=2, k=2)
    heads = lambda x: x.rearrange("p (h n) -> p h n", h=NH)
    spread = lambda x, n: x.unsqueeze(2).to_broadcast([P, NH, n])
    cumulate, neg, final = [m.le, m.ge], [m.neg_f, m.neg_b], [m.last, m.first]
    bank = lambda d, j: m.ps[:, 4 * d + j, :]
    KSCALE = DK ** -0.5

    with Stage(nc, "mlstm") as st:
        pool_, dve_, act_, pe_ = ([Order(st.sem(f"{e}_done{d}"), s) for d in range(2)] for e, s in (
            ("pool", "qk"),
            ("dve", "diag masked amax mu shifted a_ei b_t m_t a_m last blm a_wk a_dec m_new qs kw S neg_den den r "
                    "h0 h1 h2 h3 C0 C1 C2 C3 n_dec n_new"),
            ("act", "qT kT E exps ST qsT"),
            ("pe", "tq tk rows QK last tS tqs num den dC dn")))
        pre, cleared, stored, state_in, gate_in = (
            st.sem(n) for n in ("pre", "cleared", "stored", "state_in", "gate_in"))
        block = st.block()

        @block.sync
        def _(sp):
            sp.dma_start(bg, a["mlstm_b_gate"].partition_broadcast(P)).then_inc(gate_in, 16)
            with nc.allow_non_contiguous_dma(reason="normaliser rows of 4 bytes"):
                for d in range(2):
                    sp.wait_ge(dve_[d].sem, dve_[d].at(0, "n_new"))
                    sp.dma_start(a["new_C"][0, d].rearrange("h k v -> k h v"), heads(C[d])).then_inc(stored, 16)
                    sp.dma_start(a["new_n"][0, d].rearrange("h k -> k h"), n_st[d]).then_inc(stored, 16)
                    sp.dma_start(a["new_m"][0, d:d + 1], mprev[d][0:1, :]).then_inc(stored, 16)
                sp.wait_ge(stored, 96)
                for d in range(2):
                    sp.dma_start(heads(C[d]), a["state_mlstm_C"][0, d].rearrange("h k v -> k h v")).then_inc(state_in, 16)
                    sp.dma_start(n_st[d], a["state_mlstm_n"][0, d].rearrange("h k -> k h")).then_inc(state_in, 16)
                    sp.dma_start(mprev[d], a["state_mlstm_m"][0, d].partition_broadcast(P)).then_inc(state_in, 16)

        @block.gpsimd
        def _(pool):
            pool.memset(m.H, 0.0).then_inc(cleared, 1)
            for d in range(2):
                pool.memset(C[d], 0.0).then_inc(cleared, 1)
                pool.memset(n_st[d], 0.0).then_inc(cleared, 1)
                pool.memset(mprev[d], 0.0).then_inc(cleared, 1)

            def round_(i):
                for d, t in enumerate(tiles_of(pool, i)):
                    if not isinstance(i, int):
                        pool.wait_ge(pe_[d].sem, pe_[d].at(i - 1, "tk"))
                    pool.tensor_copy(qk[d], m.proj[:, t, 0:2 * HALF]).then_inc(pool_[d].sem, 1)

            round_(0)
            with pool.Fori(1, NT) as i:
                round_(i)

        @block.scalar
        def _(act):
            act.wait_ge(pre, 1)
            for d in range(2):
                act.activation(tmp[d].rearrange("p (t h) -> p t h", t=NT), G[:, d, 1], ACT.Abs).then_inc(pre, 1)
            act.wait_ge(pre, 3)
            for d in range(2):
                act.activation(tmp[d], tmp[d], ACT.Exp, scale=-1.0).then_inc(pre, 1)
            act.wait_ge(pre, 5)
            for d in range(2):
                act.activation(tmp[d], tmp[d], ACT.Ln, bias=1.0).then_inc(pre, 1)

            def round_(i):
                first = isinstance(i, int)
                for d in range(2):
                    act.wait_ge(pe_[d].sem, pe_[d].at(i, "tq"))
                    act.copy(qT[d], bank(d, 0)).then_inc(act_[d].sem, 1)
                for d in range(2):
                    act.wait_ge(pe_[d].sem, pe_[d].at(i, "tk"))
                    act.mul(kT[d], bank(d, 1), KSCALE).then_inc(act_[d].sem, 1)
                for d in range(2):
                    act.wait_ge(dve_[d].sem, dve_[d].at(i, "shifted"))
                    act.activation(E[d], E[d], ACT.Exp).then_inc(act_[d].sem, 1)
                for d in range(2):
                    act.wait_ge(dve_[d].sem, dve_[d].at(i, "a_dec"))
                    act.activation(args[d], args[d], ACT.Exp).then_inc(act_[d].sem, 1)
                for d in range(2):
                    act.wait_ge(pe_[d].sem, pe_[d].at(i, "tS"))
                    act.copy(ST[d], bank(d, 0)).then_inc(act_[d].sem, 1)
                for d in range(2):
                    act.wait_ge(pe_[d].sem, pe_[d].at(i, "tqs"))
                    act.copy(qsT[d], bank(d, 1)).then_inc(act_[d].sem, 1)

            round_(0)
            with act.Fori(1, NT) as i:
                round_(i)

        @block.tensor
        def _(pe):
            pe.wait_ge(pre, 9)
            for d in range(2):
                mm = pe.matmul(m.ps[:, 0, d * NT * NH:(d + 1) * NT * NH], cumulate[d], lf[d], start=True, stop=True)
                mm.then_inc(pre, 1)

            def round_(i):
                first = isinstance(i, int)
                tiles = tiles_of(pe, i)
                for d in range(2):
                    pe.wait_ge(pool_[d].sem, pool_[d].at(i, "qk"))
                    if first:
                        pe.wait_ge(pre, 15)
                    else:
                        pe.wait_ge(dve_[d].sem, dve_[d].at(i - 1, "C3"))
                    for n in range(2):
                        for h in range(NH):
                            tr = pe.transpose(bank(d, n)[:, h * P:(h + 1) * P],
                                              qk[d][:, n * HALF + h * P:n * HALF + (h + 1) * P], m.ident)
                        tr.then_inc(pe_[d].sem, 1)
                for d in range(2):
                    pe.wait_ge(dve_[d].sem, dve_[d].at(i, "diag"))
                    pe.matmul(bank(d, 2), m.ones, ST[d], start=True, stop=True).then_inc(pe_[d].sem, 1)
                for d in range(2):
                    pe.wait_ge(act_[d].sem, act_[d].at(i, "kT"))
                    for h in range(NH):
                        mm = pe.matmul(bank(d, 3)[:, h * P:(h + 1) * P], qT[d][:, h * P:(h + 1) * P],
                                       kT[d][:, h * P:(h + 1) * P], start=True, stop=True)
                    mm.then_inc(pe_[d].sem, 1)
                for d in range(2):
                    pe.wait_ge(dve_[d].sem, dve_[d].at(i, "m_t"))
                    pe.matmul(bank(d, 2)[:, 0:8], final[d], bm[d], start=True, stop=True).then_inc(pe_[d].sem, 1)
                for d in range(2):
                    pe.wait_ge(dve_[d].sem, dve_[d].at(i, "S"))
                    for h in range(NH):
                        tr = pe.transpose(bank(d, 0)[:, h * P:(h + 1) * P], E[d][:, h * P:(h + 1) * P], m.ident)
                    tr.then_inc(pe_[d].sem, 1)
                    for h in range(NH):
                        tr = pe.transpose(bank(d, 1)[:, h * P:(h + 1) * P], qs[d][:, h * P:(h + 1) * P], m.ident)
                    tr.then_inc(pe_[d].sem, 1)
                for d, t in enumerate(tiles):
                    pe.wait_ge(act_[d].sem, act_[d].at(i, "qsT"))
                    for h in range(NH):
                        out = bank(d, 2 + h // 2)[:, (h % 2) * DV:(h % 2 + 1) * DV]
                        pe.matmul(out, ST[d][:, h * P:(h + 1) * P],
                                  m.proj[:, t, 2 * HALF + h * DV:2 * HALF + (h + 1) * DV], start=True, stop=False)
                        mm = pe.matmul(out, qsT[d][:, h * P:(h + 1) * P], C[d][:, h * DV:(h + 1) * DV], start=False, stop=True)
                    mm.then_inc(pe_[d].sem, 1)
                    for h in range(NH):
                        pe.matmul(bank(d, 0)[:, h:h + 1], ST[d][:, h * P:(h + 1) * P], m.ones[:, 0:1], start=True, stop=False)
                        mm = pe.matmul(bank(d, 0)[:, h:h + 1], qsT[d][:, h * P:(h + 1) * P], n_st[d][:, h:h + 1],
                                       start=False, stop=True)
                    mm.then_inc(pe_[d].sem, 1)
                for d, t in enumerate(tiles):
                    pe.wait_ge(dve_[d].sem, dve_[d].at(i, "den"))
                    for h in range(NH):
                        mm = pe.matmul(bank(d, h // 2)[:, (h % 2) * DV:(h % 2 + 1) * DV], kw[d][:, h * P:(h + 1) * P],
                                       m.proj[:, t, 2 * HALF + h * DV:2 * HALF + (h + 1) * DV], start=True, stop=True)
                    mm.then_inc(pe_[d].sem, 1)
                for d in range(2):
                    pe.wait_ge(dve_[d].sem, dve_[d].at(i, "h3"))
                    for h in range(NH):
                        mm = pe.matmul(bank(d, 2)[:, h:h + 1], kw[d][:, h * P:(h + 1) * P], m.ones[:, 0:1],
                                       start=True, stop=True)
                    mm.then_inc(pe_[d].sem, 1)

            round_(0)
            with pe.Fori(1, NT) as i:
                round_(i)

        @block.vector
        def _(dve):
            dve.wait_ge(gate_in, 16)
            dve.tensor_tensor(m.gates[:, :, 0:16], m.gates[:, :, 0:16], bg.unsqueeze(1).to_broadcast([P, NT, 16]),
                              ALU.add).then_inc(pre, 1)
            dve.wait_ge(pre, 7)
            for d in range(2):
                dve.scalar_tensor_tensor(out=lf[d].rearrange("p (t h) -> p t h", t=NT), in0=G[:, d, 1], scalar=0.0,
                                         in1=tmp[d].rearrange("p (t h) -> p t h", t=NT),
                                         op0=ALU.min, op1=ALU.subtract).then_inc(pre, 1)
            dve.wait_ge(pre, 11)
            for d in range(2):
                dve.tensor_copy(b_all[d].rearrange("p t h -> p (t h)"),
                                m.ps[:, 0, d * NT * NH:(d + 1) * NT * NH]).then_inc(pre, 1)
            dve.wait_ge(pre, 13)
            for d in range(2):
                dve.tensor_tensor(a_all[d], G[:, d, 0], b_all[d], ALU.subtract).then_inc(pre, 1)
            dve.wait_ge(pre, 15)
            dve.wait_ge(cleared, 7)

            def round_(i):
                first = isinstance(i, int)
                tiles = tiles_of(dve, i)

                def own(d, step):
                    dve.wait_ge(dve_[d].sem, dve_[d].at(i, step))

                for d, t in enumerate(tiles):
                    if not first:
                        dve.wait_ge(pe_[d].sem, pe_[d].at(i - 1, "dn"))
                        dve.wait_ge(dve_[d].sem, dve_[d].at(i - 1, "n_new"))
                    dve.tensor_tensor(heads(ST[d]), m.ident.unsqueeze(1).to_broadcast([P, NH, P]),
                                      spread(a_all[d][:, t, :], P), ALU.mult).then_inc(dve_[d].sem, 1)
                for d in range(2):
                    dve.wait_ge(pe_[d].sem, pe_[d].at(i, "rows"))
                    dve.tensor_tensor(heads(E[d]), heads(bank(d, 2)), neg[d].unsqueeze(1).to_broadcast([P, NH, P]),
                                      ALU.add).then_inc(dve_[d].sem, 1)
                for d in range(2):
                    own(d, "masked")
                    dve.tensor_reduce(amax[d], heads(E[d]), AX.X, ALU.max).then_inc(dve_[d].sem, 1)
                for d in range(2):
                    own(d, "amax")
                    if not first:
                        dve.wait_ge(state_in, 96)
                    dve.tensor_tensor(mu[d], amax[d], mprev[d], ALU.max).then_inc(dve_[d].sem, 1)
                for d, t in enumerate(tiles):
                    own(d, "mu")
                    dve.tensor_tensor(heads(E[d]), heads(E[d]), spread(mu[d], P), ALU.subtract).then_inc(dve_[d].sem, 1)
                    dve.tensor_tensor(args[d][:, 0:4], mprev[d], mu[d], ALU.subtract).then_inc(dve_[d].sem, 1)
                    dve.tensor_copy(bm[d][:, 0:4], b_all[d][:, t, :]).then_inc(dve_[d].sem, 1)
                    dve.tensor_tensor(bm[d][:, 4:8], b_all[d][:, t, :], mu[d], ALU.add).then_inc(dve_[d].sem, 1)
                for d in range(2):
                    own(d, "m_t")
                    dve.tensor_scalar(args[d][:, 4:8], bm[d][:, 4:8], -1.0, None, ALU.mult).then_inc(dve_[d].sem, 1)
                for d in range(2):
                    dve.wait_ge(pe_[d].sem, pe_[d].at(i, "last"))
                    dve.tensor_copy(last[d], bank(d, 2)[:, 0:8]).then_inc(dve_[d].sem, 1)
                for d in range(2):
                    own(d, "last")
                    dve.tensor_tensor(blm[d], last[d][:, 0:4], last[d][:, 4:8], ALU.subtract).then_inc(dve_[d].sem, 1)
                for d, t in enumerate(tiles):
                    own(d, "blm")
                    dve.tensor_tensor(args[d][:, 8:12], a_all[d][:, t, :], blm[d], ALU.add).then_inc(dve_[d].sem, 1)
                    dve.tensor_tensor(args[d][:, 12:16], mprev[d], blm[d], ALU.add).then_inc(dve_[d].sem, 1)
                for d in range(2):
                    own(d, "a_dec")
                    dve.tensor_copy(mprev[d], last[d][:, 4:8]).then_inc(dve_[d].sem, 1)
                for d, t in enumerate(tiles):
                    dve.wait_ge(act_[d].sem, act_[d].at(i, "exps"))
                    dve.tensor_tensor(heads(qs[d]), heads(m.proj[:, t, 0:HALF]), spread(args[d][:, 0:4], P),
                                      ALU.mult).then_inc(dve_[d].sem, 1)
                    dve.scalar_tensor_tensor(out=heads(kw[d]), in0=heads(m.proj[:, t, HALF:2 * HALF]), scalar=KSCALE,
                                             in1=spread(args[d][:, 8:12], P), op0=ALU.mult, op1=ALU.mult)\
                        .then_inc(dve_[d].sem, 1)
                for d in range(2):
                    dve.wait_ge(pe_[d].sem, pe_[d].at(i, "QK"))
                    dve.wait_ge(act_[d].sem, act_[d].at(i, "E"))
                    dve.tensor_tensor(E[d], bank(d, 3), E[d], ALU.mult).then_inc(dve_[d].sem, 1)
                for d in range(2):
                    dve.wait_ge(pe_[d].sem, pe_[d].at(i, "den"))
                    dve.scalar_tensor_tensor(out=den[d], in0=bank(d, 0)[:, 0:4], scalar=-1.0, in1=args[d][:, 4:8],
                                             op0=ALU.mult, op1=ALU.max).then_inc(dve_[d].sem, 1)
                for d in range(2):
                    own(d, "neg_den")
                    dve.tensor_tensor(den[d], bank(d, 0)[:, 0:4], den[d], ALU.max).then_inc(dve_[d].sem, 1)
                for d in range(2):
                    own(d, "den")
                    dve.reciprocal(den[d], den[d]).then_inc(dve_[d].sem, 1)
                for d, t in enumerate(tiles):
                    own(d, "r")
                    if first and d == 1:
                        dve.wait_ge(dve_[0].sem, dve_[0].at(i, "h3"))
                    for h in range(NH):
                        out = m.H[:, t, h * DV:(h + 1) * DV]
                        dve.scalar_tensor_tensor(out=out, in0=bank(d, 2 + h // 2)[:, (h % 2) * DV:(h % 2 + 1) * DV],
                                                 scalar=den[d][:, h:h + 1], in1=out, op0=ALU.mult, op1=ALU.add)\
                            .then_inc(dve_[d].sem, 1)
                for d in range(2):
                    dve.wait_ge(pe_[d].sem, pe_[d].at(i, "dC"))
                    for h in range(NH):
                        state = C[d][:, h * DV:(h + 1) * DV]
                        dve.scalar_tensor_tensor(out=state, in0=state, scalar=args[d][:, 12 + h:13 + h],
                                                 in1=bank(d, h // 2)[:, (h % 2) * DV:(h % 2 + 1) * DV],
                                                 op0=ALU.mult, op1=ALU.add).then_inc(dve_[d].sem, 1)
                    dve.tensor_tensor(n_st[d], n_st[d], args[d][:, 12:16], ALU.mult).then_inc(dve_[d].sem, 1)
                for d in range(2):
                    own(d, "n_dec")
                    dve.wait_ge(pe_[d].sem, pe_[d].at(i, "dn"))
                    dve.tensor_tensor(n_st[d], n_st[d], bank(d, 2)[:, 0:4], ALU.add).then_inc(dve_[d].sem, 1)

            round_(0)
            with dve.Fori(1, NT) as i:
                round_(i)


NORM = "st0 st1 mv eps rstd centred gained"


def layer_norm(nc, dve, m, order, act_order, i, y, out, ready, passed):
    stats, mv, rs = m.stat[:, 0:12], m.stat[:, 12:14], m.stat[:, 14:15]
    own = lambda step: dve.wait_ge(order.sem, order.at(i, step))
    own(ready)
    for h in range(2):
        dve.bn_stats(stats[:, 6 * h:6 * h + 6], y[:, h * HALF:(h + 1) * HALF]).then_inc(order.sem, 1)
    own("st1")
    dve.sem_inc(passed, 1)
    dve.bn_aggr(mv, stats).then_inc(order.sem, 1)
    own("mv")
    dve.tensor_scalar(rs, mv[:, 1:2], EPS, None, ALU.add).then_inc(order.sem, 1)
    dve.wait_ge(act_order.sem, act_order.at(i, "sqrt"))
    dve.reciprocal(rs, rs).then_inc(order.sem, 1)
    own("rstd")
    dve.tensor_scalar(y, y, mv[:, 0:1], rs, ALU.subtract, ALU.mult).then_inc(order.sem, 1)
    own("centred")
    dve.tensor_tensor(y, y, m.lnw[:, 0, :], ALU.mult).then_inc(order.sem, 1)
    own("gained")
    dve.tensor_tensor(out, y, m.lnw[:, 1, :], ALU.add).then_inc(order.sem, 1)


def layer_norm_sqrt(act, m, order, act_order, i):
    act.wait_ge(order.sem, order.at(i, "eps"))
    act.activation(m.stat[:, 14:15], m.stat[:, 14:15], ACT.Sqrt).then_inc(act_order.sem, 1)


def mixer_output(nc, m, a, layer):
    w = a[("mlstm_w_out", "gla_w_out")[layer]].rearrange("(k p) n -> p k n", p=P)
    norm_w = a[("mlstm_norm_w", "gla_norm_w")[layer]]
    W = m.wrk[:, 0:KD * D].rearrange("p (k n) -> p k n", k=KD)
    nw = m.mod[:, 0, 0, :]
    z = m.big[:, NT * NP_:NT * NP_ + D]
    st6 = m.stat[:, 16:40]
    mv = m.scr[:, 0:8].rearrange("p (h s) -> p h s", h=NH)
    var = m.scr[:, 8:12]
    with Stage(nc, f"out{layer}") as st:
        head = Order(st.sem("head"), "b0 b1 b2 b3 a0 a1 a2 a3 sq ms eps rstd n0 n1 n2 n3 weighed gated")
        rest = Order(st.sem("rest"), "scaled added " + NORM + " done")
        head_act, rest_act = Order(st.sem("head_act"), "sqrt"), Order(st.sem("rest_act"), "sqrt")
        loaded, transposed, copied, product = (st.sem(n) for n in ("loaded", "transposed", "copied", "product"))
        passed = st.sem("passed")
        block = st.block()

        @block.sync
        def _(sp):
            n = load_rows(sp, m, a, layer, 0, (2,), "mix", loaded)
            for h in range(HV // norm_w.shape[0]):
                s = norm_w.shape[0]
                sp.dma_start(nw[:, h * s:(h + 1) * s], norm_w.partition_broadcast(P)).then_inc(loaded, 16)
            sp.dma_start(W, w).then_inc(loaded, 16)

        n_loads = 4 + HV // norm_w.shape[0] + 1

        @block.tensor
        def _(pe):
            def tile(t):
                first = is_first(t)
                pe.wait_ge(head.sem, head.at(t, "gated"))
                if not first:
                    pe.wait_ge(copied, t)
                for k in range(KD):
                    tr = pe.transpose(m.ps[:, k // 4, (k % 4) * P:(k % 4 + 1) * P], m.y[:, k * P:(k + 1) * P], m.ident)
                tr.then_inc(transposed, 1)
                if not first:
                    pe.wait_ge(rest.sem, rest.at(t - 1, "scaled"))
                pe.wait_ge(copied, t + 1)
                if first:
                    pe.wait_ge(loaded, 16 * n_loads)
                for n in range(2):
                    for k in range(KD):
                        mm = pe.matmul(m.ps[:, 2 + n, :], m.yT[:, k, :], W[:, k, n * HALF:(n + 1) * HALF],
                                       start=k == 0, stop=k == KD - 1)
                mm.then_inc(product, 1)

            tile(0)
            with pe.Fori(1, NT) as t:
                tile(t)

        @block.scalar
        def _(act):
            def sqrt_head(t):
                act.wait_ge(head.sem, head.at(t, "eps"))
                act.activation(var, var, ACT.Sqrt).then_inc(head_act.sem, 1)

            def evacuate(t):
                act.wait_ge(transposed, t + 1)
                if not is_first(t):
                    act.wait_ge(product, t)
                act.copy(m.yT[:].rearrange("p k n -> p (k n)"), m.ps[:, 0:2, :].rearrange("p b n -> p (b n)"))\
                    .then_inc(copied, 1)

            sqrt_head(0)
            evacuate(0)
            with act.Fori(1, NT) as t:
                sqrt_head(t)
                layer_norm_sqrt(act, m, rest, rest_act, t - 1)
                evacuate(t)
            layer_norm_sqrt(act, m, rest, rest_act, NT - 1)

        @block.vector
        def _(dve):
            def head_norm(t):
                own = lambda step: dve.wait_ge(head.sem, head.at(t, step))
                hh = lambda h: m.H[:, t, h * DV:(h + 1) * DV]
                for h in range(NH):
                    dve.bn_stats(st6[:, 6 * h:6 * h + 6], hh(h)).then_inc(head.sem, 1)
                own("b3")
                dve.sem_inc(passed, 1)
                for h in range(NH):
                    dve.bn_aggr(mv[:, h, :], st6[:, 6 * h:6 * h + 6]).then_inc(head.sem, 1)
                own("a3")
                dve.tensor_tensor(var, mv[:, :, 0], mv[:, :, 0], ALU.mult).then_inc(head.sem, 1)
                own("sq")
                dve.scalar_tensor_tensor(out=var, in0=var, scalar=float(layer == 1), in1=mv[:, :, 1], op0=ALU.mult,
                                         op1=ALU.add).then_inc(head.sem, 1)
                own("ms")
                dve.tensor_scalar(var, var, EPS, None, ALU.add).then_inc(head.sem, 1)
                dve.wait_ge(head_act.sem, head_act.at(t, "sqrt"))
                dve.reciprocal(var, var).then_inc(head.sem, 1)
                own("rstd")
                if not is_first(t):
                    dve.wait_ge(transposed, t)
                for h in range(NH):
                    y = m.y[:, h * DV:(h + 1) * DV]
                    if layer == 0:
                        ins = dve.tensor_scalar(y, hh(h), mv[:, h, 0:1], var[:, h:h + 1], ALU.subtract, ALU.mult)
                    else:
                        ins = dve.tensor_scalar(y, hh(h), var[:, h:h + 1], None, ALU.mult)
                    ins.then_inc(head.sem, 1)
                own("n3")
                dve.tensor_tensor(m.y[:], m.y[:], nw, ALU.mult).then_inc(head.sem, 1)
                own("weighed")
                dve.tensor_tensor(m.y[:], m.y[:], m.proj[:, t, 4 * HALF:6 * HALF], ALU.mult).then_inc(head.sem, 1)

            def residual(t, c):
                dve.wait_ge(product, t + 1)
                if not is_first(t):
                    dve.wait_ge(rest.sem, rest.at(t - 1, "done"))
                dve.tensor_tensor(z, m.ps[:, 2:4, :].rearrange("p b n -> p (b n)"), m.mod[:, 2, c, :],
                                  ALU.mult).then_inc(rest.sem, 1)
                dve.wait_ge(rest.sem, rest.at(t, "scaled"))
                dve.scalar_tensor_tensor(out=z, in0=m.X[:, t, :], scalar=ALPHA, in1=z, op0=ALU.mult,
                                         op1=ALU.add).then_inc(rest.sem, 1)
                layer_norm(nc, dve, m, rest, rest_act, t, z, m.X[:, t, :], "added", passed)

            dve.wait_ge(loaded, 16 * n_loads)
            head_norm(0)
            head_norm(1)
            residual(0, 0)
            with dve.Fori(2, NT) as t:
                head_norm(t)
                residual(t - 1, 1)
            residual(NT - 1, 1)


def load_rows(sp, m, a, layer, first, which, ln, sem):
    for n in which:
        for c in range(2):
            row = a["rows"][layer, c, (first + n) * D:(first + n + 1) * D]
            sp.dma_start(m.mod[:, n, c, :], row.partition_broadcast(P)).then_inc(sem, 16)
    for n, name in enumerate(("g", "b")):
        sp.dma_start(m.lnw[:, n, :], a[f"ln_{ln}_{name}"][layer].partition_broadcast(P)).then_inc(sem, 16)


def gla_scan(nc, m, a):
    base = [m.wrk[:, 0:8192], m.mod[:].rearrange("p a c n -> p (a c n)")]
    at = [0]

    def part(n):
        at[0] += n
        return [b[:, at[0] - n:at[0]] for b in base]

    KB = part(NB * HALF)
    qT, kT, la, bcS, full, ql, kl, AT = (part(HALF) for _ in range(8))
    S = [m.wrk[:, 7168:8192], m.wrk[:, 13312:14336]]
    x = AT
    g16 = [m.scr[:, 16 * d:16 * d + 16] for d in range(2)]
    decay = [m.scr[:, 32 + 4 * d:36 + 4 * d] for d in range(2)]
    gT = [m.y[0:RANK, P * d:P * (d + 1)] for d in range(2)]
    w2 = [m.yT[:].rearrange("p k n -> p (k n)")[0:RANK, HALF * d:HALF * (d + 1)] for d in range(2)]
    bg = [m.big[:, NT * NP_ + HALF * d:NT * NP_ + HALF * (d + 1)] for d in range(2)]
    qk = [m.qk[:, 0:2 * HALF], m.qk[:, 2 * HALF:4 * HALF]]
    heads = lambda v: v.rearrange("p (h n) -> p h n", h=NH)
    blocks = lambda v: v.rearrange("p (h b n) -> p h b n", h=NH, b=NB)
    cumulate, rest16, causal = [m.le16, m.ge16], [m.gt16, m.lt16], [m.le, m.ge]
    final = [P - 1, 0]
    bank = lambda d, j: m.ps[:, 4 * d + j, :]
    QSCALE = DK ** -0.5

    def keys(d, i):
        return slice(0, BL * (i + 1)) if d == 0 else slice(BL * i, P)

    def before(d, i):
        t = BL * i - 1 if d == 0 else BL * (i + 1)
        return t if 0 <= t < P else None

    def start_block(d):
        return 0 if d == 0 else NB - 1

    with Stage(nc, "gla") as st:
        pool_, dve_, act_, pe_ = ([Order(st.sem(f"{e}_done{d}"), s) for d in range(2)] for e, s in (
            ("pool", "qk"),
            ("dve", "gate x la ql0 ql kb0 kb1 kb2 kb3 decay qd qf kl keys0 keys1 keys2 keys3 A o S0 S1 S2 S3"),
            ("act", "qT kT gT abs exp ln bcS full kl ql kb0 kb1 kb2 kb3"),
            ("pe", "tq tk tg gates bc suffix A o dS")))
        cleared, stored, state_in, loaded = (st.sem(n) for n in ("cleared", "stored", "state_in", "loaded"))
        block = st.block()

        @block.sync
        def _(sp):
            for d in range(2):
                sp.dma_start(w2[d], a["gla_w_gate2"][d]).then_inc(loaded, 16)
                sp.dma_start(bg[d], a["gla_b_gate2"][d].partition_broadcast(P)).then_inc(loaded, 16)
            for d in range(2):
                sp.wait_ge(dve_[d].sem, dve_[d].at(0, "S3"))
                sp.dma_start(a["new_S"][0, d].rearrange("h k v -> k h v"), heads(S[d])).then_inc(stored, 16)
            sp.wait_ge(stored, 32)
            for d in range(2):
                sp.dma_start(heads(S[d]), a["state_gla_S"][0, d].rearrange("h k v -> k h v")).then_inc(state_in, 16)

        @block.gpsimd
        def _(pool):
            for d in range(2):
                pool.memset(S[d], 0.0).then_inc(cleared, 1)
                pool.memset(KB[d], 0.0).then_inc(cleared, 1)
            pool.memset(m.H, 0.0).then_inc(cleared, 1)

            def round_(i):
                for d, t in enumerate(tiles_of(pool, i)):
                    if not is_first(i):
                        pool.wait_ge(pe_[d].sem, pe_[d].at(i - 1, "tk"))
                    pool.tensor_copy(qk[d], m.proj[:, t, 0:2 * HALF]).then_inc(pool_[d].sem, 1)

            round_(0)
            with pool.Fori(1, NT) as i:
                round_(i)

        @block.scalar
        def _(act):
            def round_(i):
                def after_pe(d, step):
                    act.wait_ge(pe_[d].sem, pe_[d].at(i, step))

                def own(d, step):
                    act.wait_ge(act_[d].sem, act_[d].at(i, step))

                for d in range(2):
                    after_pe(d, "tq")
                    if not is_first(i):
                        act.wait_ge(dve_[d].sem, dve_[d].at(i - 1, "keys3"))
                    act.mul(qT[d], bank(d, 0), QSCALE).then_inc(act_[d].sem, 1)
                    after_pe(d, "tk")
                    act.copy(kT[d], bank(d, 1)).then_inc(act_[d].sem, 1)
                for d in range(2):
                    after_pe(d, "tg")
                    act.copy(gT[d], bank(d, 2)[0:RANK, 0:P]).then_inc(act_[d].sem, 1)
                for d in range(2):
                    act.wait_ge(dve_[d].sem, dve_[d].at(i, "x"))
                    act.activation(la[d], x[d], ACT.Abs).then_inc(act_[d].sem, 1)
                for d in range(2):
                    own(d, "abs")
                    act.activation(la[d], la[d], ACT.Exp, scale=-1.0).then_inc(act_[d].sem, 1)
                for d in range(2):
                    own(d, "exp")
                    act.activation(la[d], la[d], ACT.Ln, bias=1.0).then_inc(act_[d].sem, 1)
                for d in range(2):
                    after_pe(d, "bc")
                    act.copy(bcS[d], bank(d, 2)).then_inc(act_[d].sem, 1)
                    act.activation(full[d], bank(d, 2), ACT.Exp).then_inc(act_[d].sem, 1)
                    after_pe(d, "suffix")
                    act.activation(kl[d], bank(d, 3), ACT.Exp).then_inc(act_[d].sem, 1)
                for d in range(2):
                    act.wait_ge(dve_[d].sem, dve_[d].at(i, "ql"))
                    act.activation(ql[d], ql[d], ACT.Exp).then_inc(act_[d].sem, 1)
                    for j in range(NB):
                        act.wait_ge(dve_[d].sem, dve_[d].at(i, f"kb{j}"))
                        kb = heads(KB[d][:, j * HALF:(j + 1) * HALF])[:, :, keys(d, j)]
                        act.activation(kb, kb, ACT.Exp).then_inc(act_[d].sem, 1)

            round_(0)
            with act.Fori(1, NT) as i:
                round_(i)

        @block.tensor
        def _(pe):
            pe.wait_ge(loaded, 64)

            def round_(i):
                tiles = tiles_of(pe, i)
                for d in range(2):
                    pe.wait_ge(pool_[d].sem, pool_[d].at(i, "qk"))
                    if not is_first(i):
                        pe.wait_ge(dve_[d].sem, dve_[d].at(i - 1, "S3"))
                    for n in range(2):
                        for h in range(NH):
                            tr = pe.transpose(bank(d, n)[:, h * P:(h + 1) * P],
                                              qk[d][:, n * HALF + h * P:n * HALF + (h + 1) * P], m.ident)
                        tr.then_inc(pe_[d].sem, 1)
                for d in range(2):
                    pe.wait_ge(dve_[d].sem, dve_[d].at(i, "gate"))
                    pe.transpose(bank(d, 2)[0:RANK, 0:P], g16[d], m.ident).then_inc(pe_[d].sem, 1)
                for d in range(2):
                    pe.wait_ge(act_[d].sem, act_[d].at(i, "gT"))
                    pe.matmul(bank(d, 3), gT[d], w2[d], start=True, stop=True).then_inc(pe_[d].sem, 1)
                for d in range(2):
                    pe.wait_ge(dve_[d].sem, dve_[d].at(i, "la"))
                    for h in range(NH):
                        mm = pe.matmul(bank(d, 2)[:, h * P:(h + 1) * P], la[d][:, h * P:(h + 1) * P], cumulate[d],
                                       start=True, stop=True)
                    mm.then_inc(pe_[d].sem, 1)
                    pe.matmul(bank(d, 3), rest16[d], la[d], start=True, stop=True).then_inc(pe_[d].sem, 1)
                for d in range(2):
                    pe.wait_ge(dve_[d].sem, dve_[d].at(i, "keys3"))
                    for h in range(NH):
                        for j in range(NB):
                            mm = pe.matmul(bank(d, 0)[:, h * P + j * BL:h * P + (j + 1) * BL],
                                           KB[d][:, j * HALF + h * P:j * HALF + (h + 1) * P],
                                           ql[d][:, h * P + j * BL:h * P + (j + 1) * BL], start=True, stop=True)
                    mm.then_inc(pe_[d].sem, 1)
                if not is_first(i):
                    pe.wait_ge(state_in, 32)
                for d, t in enumerate(tiles):
                    pe.wait_ge(act_[d].sem, act_[d].at(i, "kl"))
                    pe.wait_ge(dve_[d].sem, dve_[d].at(i, "A"))
                    for h in range(NH):
                        out = bank(d, 2 + h // 2)[:, (h % 2) * DV:(h % 2 + 1) * DV]
                        pe.matmul(out, AT[d][:, h * P:(h + 1) * P],
                                  m.proj[:, t, 2 * HALF + h * DV:2 * HALF + (h + 1) * DV], start=True, stop=False)
                        mm = pe.matmul(out, full[d][:, h * P:(h + 1) * P], S[d][:, h * DV:(h + 1) * DV],
                                       start=False, stop=True)
                    mm.then_inc(pe_[d].sem, 1)
                for d, t in enumerate(tiles):
                    for h in range(NH):
                        mm = pe.matmul(bank(d, h // 2)[:, (h % 2) * DV:(h % 2 + 1) * DV], kl[d][:, h * P:(h + 1) * P],
                                       m.proj[:, t, 2 * HALF + h * DV:2 * HALF + (h + 1) * DV], start=True, stop=True)
                    mm.then_inc(pe_[d].sem, 1)

            round_(0)
            with pe.Fori(1, NT) as i:
                round_(i)

        @block.vector
        def _(dve):
            dve.wait_ge(cleared, 5)
            dve.wait_ge(loaded, 64)

            def round_(i):
                tiles = tiles_of(dve, i)

                def after_act(d, step):
                    dve.wait_ge(act_[d].sem, act_[d].at(i, step))

                for d, t in enumerate(tiles):
                    if not is_first(i):
                        dve.wait_ge(dve_[d].sem, dve_[d].at(i - 1, "S3"))
                    dve.tensor_copy(g16[d], m.gates[:, t, RANK * d:RANK * (d + 1)]).then_inc(dve_[d].sem, 1)
                for d in range(2):
                    dve.wait_ge(pe_[d].sem, pe_[d].at(i, "gates"))
                    dve.tensor_tensor(x[d], bank(d, 3), bg[d], ALU.add).then_inc(dve_[d].sem, 1)
                for d in range(2):
                    after_act(d, "ln")
                    dve.scalar_tensor_tensor(out=la[d], in0=x[d], scalar=0.0, in1=la[d], op0=ALU.min,
                                             op1=ALU.subtract).then_inc(dve_[d].sem, 1)
                for d in range(2):
                    after_act(d, "bcS")
                    j0 = start_block(d)
                    dve.tensor_copy(blocks(ql[d])[:, :, j0, :], blocks(bcS[d])[:, :, j0, :]).then_inc(dve_[d].sem, 1)
                    others = slice(1, NB) if d == 0 else slice(0, NB - 1)
                    edge = blocks(bcS[d])[:, :, 0:NB - 1, BL - 1] if d == 0 else blocks(bcS[d])[:, :, 1:NB, 0]
                    dve.tensor_tensor(blocks(ql[d])[:, :, others, :], blocks(bcS[d])[:, :, others, :],
                                      edge.unsqueeze(3).to_broadcast([P, NH, NB - 1, BL]), ALU.subtract)\
                        .then_inc(dve_[d].sem, 1)
                    for j in range(NB):
                        kb = heads(KB[d][:, j * HALF:(j + 1) * HALF])[:, :, keys(d, j)]
                        src = heads(bcS[d])[:, :, keys(d, j)]
                        if before(d, j) is None:
                            ins = dve.tensor_scalar(kb, src, -1.0, None, ALU.mult)
                        else:
                            edge = heads(bcS[d])[:, :, before(d, j):before(d, j) + 1]
                            ins = dve.tensor_tensor(kb, edge.to_broadcast([P, NH, src.shape[2]]), src, ALU.subtract)
                        ins.then_inc(dve_[d].sem, 1)
                for d, t in enumerate(tiles):
                    after_act(d, "full")
                    dve.tensor_copy(decay[d], heads(full[d])[:, :, final[d]]).then_inc(dve_[d].sem, 1)
                    after_act(d, "ql")
                    dve.tensor_tensor(ql[d], ql[d], qT[d], ALU.mult).then_inc(dve_[d].sem, 1)
                    dve.wait_ge(dve_[d].sem, dve_[d].at(i, "decay"))
                    dve.tensor_tensor(full[d], full[d], qT[d], ALU.mult).then_inc(dve_[d].sem, 1)
                    dve.tensor_tensor(kl[d], kl[d], m.proj[:, t, HALF:2 * HALF], ALU.mult).then_inc(dve_[d].sem, 1)
                    for j in range(NB):
                        after_act(d, f"kb{j}")
                        kb = heads(KB[d][:, j * HALF:(j + 1) * HALF])[:, :, keys(d, j)]
                        dve.tensor_tensor(kb, kb, heads(kT[d])[:, :, keys(d, j)], ALU.mult).then_inc(dve_[d].sem, 1)
                for d in range(2):
                    dve.wait_ge(pe_[d].sem, pe_[d].at(i, "A"))
                    dve.tensor_tensor(heads(AT[d]), heads(bank(d, 0)), causal[d].unsqueeze(1).to_broadcast([P, NH, P]),
                                      ALU.mult).then_inc(dve_[d].sem, 1)
                for d, t in enumerate(tiles):
                    dve.wait_ge(pe_[d].sem, pe_[d].at(i, "o"))
                    if is_first(i) and d == 1:
                        dve.wait_ge(dve_[0].sem, dve_[0].at(i, "o"))
                    out = m.H[:, t, :]
                    dve.tensor_tensor(out, out, m.ps[:, 4 * d + 2:4 * d + 4, :].rearrange("p b n -> p (b n)"),
                                      ALU.add).then_inc(dve_[d].sem, 1)
                for d in range(2):
                    dve.wait_ge(pe_[d].sem, pe_[d].at(i, "dS"))
                    for h in range(NH):
                        state = S[d][:, h * DV:(h + 1) * DV]
                        dve.scalar_tensor_tensor(out=state, in0=state, scalar=decay[d][:, h:h + 1],
                                                 in1=bank(d, h // 2)[:, (h % 2) * DV:(h % 2 + 1) * DV],
                                                 op0=ALU.mult, op1=ALU.add).then_inc(dve_[d].sem, 1)

            round_(0)
            with dve.Fori(1, NT) as i:
                dve.wait_ge(state_in, 32)
                round_(i)


ROUTE = ("mx0 mx1 ix0 ix1 cut0 cut1 mxb0 mxb1 ixb0 ixb1 idxf0 idxf cand mxc ixc cutc mxd ixd "
         "row col rc hot picked pair expert neg rsum gate")


def peer(nc, m, a, layer):
    RB = 2 * RING
    ROWS = 2 * TOPK
    PAIRS = EH // 2
    w_q = a["peer_w_q"][layer].rearrange("(k p) n -> p k n", p=P)
    u, v = (a[name].rearrange("l e n -> (l e) n") for name in ("peer_u", "peer_v"))
    at = [0]

    def part(n, buf=m.wrk):
        at[0] += n
        return buf[:, at[0] - n:at[0]]

    wq = [part(2 * KD * P).rearrange("p (k n) -> p k n", k=KD) for _ in range(2)]
    sk = part(2 * EH * NKEYS).rearrange("p (g n) -> p g n", g=EH)
    xm = part(NT * D).rearrange("p (t n) -> p t n", t=NT)
    acc = [part(D) for _ in range(2)]
    assert at[0] <= m.wrk.shape[1]
    ring = m.big[:].rearrange("p (r n) -> p r n", r=RB)
    xT = m.yT
    at[0] = 0
    small = lambda n: part(n, m.qk)
    expert = small(NT * EH * TOPK).bitcast(U32)
    gates = m.route_gate[:]
    stage = [small(TOPK).bitcast(U32) for _ in range(2)]
    qh = [m.qhT[:, 0], m.qhT[:, 1]]
    s, s2 = small(2 * NKEYS), small(2 * NKEYS)
    top = small(2 * TOPK)
    idx = small(2 * TOPK).bitcast(U32)
    idxf = small(2 * TOPK)
    cand, cand2 = small(TOPK * TOPK), m.scr[:, 0:TOPK * TOPK]
    best, pos = small(TOPK), small(TOPK).bitcast(U32)
    rc, rcf, pair = small(2 * TOPK).bitcast(U32), small(2 * TOPK), small(2 * TOPK)
    ge, neg, rsum = small(TOPK), small(1), small(1)
    act_u, tanh, wv, t1 = ([small(TOPK) for _ in range(2)] for _ in range(4))
    assert at[0] <= m.qk.shape[1]
    hot = m.hot[:]
    three = lambda ap: ap.rearrange("p (a b) -> p a b", b=TOPK)
    four = lambda ap: ap.rearrange("p (c a b) -> p c a b", c=2, b=TOPK)

    with Stage(nc, f"peer{layer}") as st:
        route = Order(st.sem("route"), ROUTE)
        route_act = Order(st.sem("route_act"), "qh scores exp")
        route_pe = Order(st.sem("route_pe"), "qh scores")
        prep = Order(st.sem("prep"), "scaled shifted")
        prep_act = Order(st.sem("prep_act"), "xT xm")
        gelu = Order(st.sem("gelu"), "sq cubic arg half weight")
        gelu_act = Order(st.sem("gelu_act"), "tanh")
        fin = Order(st.sem("fin"), "z0 z1 both scaled added " + NORM + " done")
        fin_act = Order(st.sem("fin_act"), "sqrt")
        w_full = [st.sem("w_full0"), st.sem("w_full1")]
        landed = [st.sem(f"landed{r}") for r in range(RB)]
        rows_in, used, staged, xT_done = (st.sem(n) for n in ("rows_in", "used", "staged", "xT_done"))
        passed, gather_passed, xT_held = (st.sem(n) for n in ("passed", "gather_passed", "xT_held"))
        block = st.block()
        N_ROWS_IN = 8 + 1

        @block.sync
        def _(sp):
            load_rows(sp, m, a, layer, 3, (0, 1, 2), "ffn", rows_in)
            sp.dma_start(sk, a["subkeysT"][layer]).then_inc(rows_in, 16)

            def load_pair(t, j):
                for b in range(2):
                    R = t * EH + j * 2 + b
                    if not (is_first(t) and is_first(j)):
                        sp.wait_ge(route_pe.sem, route_pe.at(R - 2, "qh"))
                    sp.dma_start(wq[b], w_q[:, :, bass.ds((j * 2 + b) * 2 * P, 2 * P)]).then_inc(w_full[b], 16)

            load_pair(0, 0)
            with sp.Fori(1, PAIRS) as j:
                load_pair(0, j)
            with sp.Fori(1, NT) as t:
                with sp.Fori(0, PAIRS) as j:
                    load_pair(t, j)

        @block.tensor
        def _(pe):
            pe.wait_ge(rows_in, 16 * N_ROWS_IN)

            def transpose(t):
                pe.wait_ge(prep.sem, prep.at(t, "shifted"))
                for k in range(KD):
                    tr = pe.transpose(m.ps[:, k // 4, (k % 4) * P:(k % 4 + 1) * P], m.y[:, k * P:(k + 1) * P], m.ident)
                tr.then_inc(xT_done, 1)
                pe.wait_ge(prep_act.sem, prep_act.at(t, "xT"))

            def heads(t, j):
                for b in range(2):
                    R = t * EH + j * 2 + b
                    pe.wait_ge(w_full[b], (t * PAIRS + j) * 16 + 16)
                    if not (is_first(t) and is_first(j)):
                        pe.wait_ge(route_act.sem, route_act.at(R - 2, "scores"))
                    for p in range(2):
                        for k in range(KD):
                            mm = pe.matmul(m.ps[:, 2 + b, p * P:(p + 1) * P], wq[b][:, k, p * P:(p + 1) * P], xT[:, k, :],
                                           start=k == 0, stop=k == KD - 1)
                    mm.then_inc(route_pe.sem, 1)
                    pe.wait_ge(route_act.sem, route_act.at(R, "qh"))
                    for p in range(2):
                        mm = pe.matmul(m.ps[:, 4 + b, p * P:(p + 1) * P], qh[b][:, p * P:(p + 1) * P],
                                       sk[:, j * 2 + b, p * NKEYS:(p + 1) * NKEYS], start=True, stop=True)
                    mm.then_inc(route_pe.sem, 1)

            transpose(0)
            heads(0, 0)
            with pe.Fori(1, PAIRS) as j:
                heads(0, j)
            with pe.Fori(1, NT) as t:
                transpose(t)
                pe.sem_inc(xT_held, 1)
                with pe.Fori(0, PAIRS) as j:
                    heads(t, j)

        @block.scalar
        def _(act):
            def prepare(t):
                act.wait_ge(xT_done, t + 1)
                if not is_first(t):
                    act.wait_ge(route_pe.sem, route_pe.at(t * EH - 1, "qh"))
                act.copy(xT[:].rearrange("p k n -> p (k n)"), m.ps[:, 0:2, :].rearrange("p b n -> p (b n)"))\
                    .then_inc(prep_act.sem, 1)
                act.copy(xm[:, t, :], m.y[:]).then_inc(prep_act.sem, 1)

            def scores(R, b, first):
                act.wait_ge(route_pe.sem, route_pe.at(R, "qh"))
                act.copy(qh[b], m.ps[:, 2 + b, 0:2 * P]).then_inc(route_act.sem, 1)
                act.wait_ge(route_pe.sem, route_pe.at(R, "scores"))
                if not first:
                    act.wait_ge(route.sem, route.at(R - 1, "cut1"))
                act.copy(s, m.ps[:, 4 + b, 0:2 * NKEYS]).then_inc(route_act.sem, 1)

            def exp(R):
                act.wait_ge(route.sem, route.at(R, "neg"))
                act.activation(ge, best, ACT.Exp, bias=neg, accum_out=rsum).then_inc(route_act.sem, 1)

            def tanh_(G, b):
                act.wait_ge(gelu.sem, gelu.at(G, "arg"))
                act.activation(tanh[b], t1[b], ACT.Tanh, scale=TANH_SCALE).then_inc(gelu_act.sem, 1)

            def routes(j):
                for b in range(2):
                    scores(j * 2 + b, b, is_first(j) and b == 0)
                    exp(j * 2 + b)

            prepare(0)
            routes(0)
            with act.Fori(1, PAIRS) as j:
                routes(j)
            with act.Fori(0, NT - 1) as t:
                prepare(t + 1)
                with act.Fori(0, PAIRS) as j:
                    for b in range(2):
                        G = t * EH + j * 2 + b
                        scores(G + EH, b, False)
                        tanh_(G, b)
                        exp(G + EH)
                layer_norm_sqrt(act, m, fin, fin_act, t)
            with act.Fori(0, PAIRS) as j:
                for b in range(2):
                    tanh_((NT - 1) * EH + j * 2 + b, b)
            layer_norm_sqrt(act, m, fin, fin_act, NT - 1)

        @block.gpsimd
        def _(pool):
            def groups(n):
                for b in range(2):
                    G = n * 2 + b
                    if not is_first(n):
                        pool.wait_ge(used, (G - 1) * ROWS)
                    pool.wait_ge(route.sem, route.at(G, "expert"))
                    pool.tensor_copy(stage[b], expert[:, bass.ds(G * TOPK, TOPK)]).then_inc(staged, 1)
                    pool.wait_ge(staged, G + 1)
                    pool.sem_inc(gather_passed, 1)
                    for r in range(ROWS):
                        if r % 4 == 0 and not (is_first(n) and b == 0 and r < RB):
                            pool.wait_ge(used, G * ROWS + r + 4 - RB)
                            pool.sem_inc(gather_passed, 1)
                        pool.indirect_dma_start(ring[:, r % RB, :], None, (u if r < TOPK else v),
                                                bass.IndirectOffsetOnAxis(ap=stage[b][:, r % TOPK:r % TOPK + 1], axis=0))\
                            .then_inc(landed[r % RB], 16)

            groups(0)
            with pool.Fori(1, NT * PAIRS) as n:
                groups(n)

        @block.vector
        def _(dve):
            def prepare(t, c):
                if not is_first(t):
                    dve.wait_ge(prep_act.sem, prep_act.at(t - 1, "xm"))
                dve.tensor_tensor(m.y[:], m.X[:, t, :], m.mod[:, 1, c, :], ALU.mult).then_inc(prep.sem, 1)
                dve.wait_ge(prep.sem, prep.at(t, "scaled"))
                dve.tensor_tensor(m.y[:], m.y[:], m.mod[:, 0, c, :], ALU.add).then_inc(prep.sem, 1)

            def route_head(R):
                def own(step):
                    dve.wait_ge(route.sem, route.at(R, step))

                half = lambda x, p: x[:, p * TOPK:(p + 1) * TOPK]
                key = lambda x, p: x[:, p * NKEYS:(p + 1) * NKEYS]
                dve.wait_ge(route_act.sem, route_act.at(R, "scores"))
                dve.sem_inc(passed, 1)
                for p in range(2):
                    dve.max(half(top, p)[:, 0:8], key(s, p)).then_inc(route.sem, 1)
                for p in range(2):
                    dve.wait_ge(route.sem, route.at(R, f"mx{p}"))
                    dve.sem_inc(passed, 1)
                    dve.max_index(half(idx, p)[:, 0:8], half(top, p)[:, 0:8], key(s, p)).then_inc(route.sem, 1)
                for p in range(2):
                    dve.match_replace(key(s2, p), half(top, p)[:, 0:8], key(s, p), NEG).then_inc(route.sem, 1)
                for p in range(2):
                    dve.wait_ge(route.sem, route.at(R, f"cut{p}"))
                    dve.sem_inc(passed, 1)
                    dve.max(half(top, p)[:, 8:16], key(s2, p)).then_inc(route.sem, 1)
                for p in range(2):
                    dve.wait_ge(route.sem, route.at(R, f"mxb{p}"))
                    dve.sem_inc(passed, 1)
                    dve.max_index(half(idx, p)[:, 8:16], half(top, p)[:, 8:16], key(s2, p)).then_inc(route.sem, 1)
                own("ixb1")
                dve.tensor_scalar(half(idxf, 0), half(idx, 0), float(layer * NKEYS), None, ALU.add).then_inc(route.sem, 1)
                dve.tensor_copy(half(idxf, 1), half(idx, 1)).then_inc(route.sem, 1)
                dve.tensor_tensor(three(cand), half(top, 0).unsqueeze(2).to_broadcast([P, TOPK, TOPK]),
                                  half(top, 1).unsqueeze(1).to_broadcast([P, TOPK, TOPK]), ALU.add).then_inc(route.sem, 1)
                own("cand")
                dve.sem_inc(passed, 1)
                dve.max(best[:, 0:8], cand).then_inc(route.sem, 1)
                own("mxc")
                dve.sem_inc(passed, 1)
                dve.max_index(pos[:, 0:8], best[:, 0:8], cand).then_inc(route.sem, 1)
                dve.match_replace(cand2, best[:, 0:8], cand, NEG).then_inc(route.sem, 1)
                own("cutc")
                dve.sem_inc(passed, 1)
                dve.max(best[:, 8:16], cand2).then_inc(route.sem, 1)
                own("mxd")
                dve.sem_inc(passed, 1)
                dve.max_index(pos[:, 8:16], best[:, 8:16], cand2).then_inc(route.sem, 1)
                own("ixd")
                dve.tensor_scalar(half(rc, 0), pos, 4, None, ALU.logical_shift_right).then_inc(route.sem, 1)
                dve.tensor_scalar(half(rc, 1), pos, TOPK - 1, None, ALU.bitwise_and).then_inc(route.sem, 1)
                own("col")
                dve.tensor_copy(rcf, rc).then_inc(route.sem, 1)
                own("rc")
                dve.tensor_tensor(four(hot), three(rcf).unsqueeze(3).to_broadcast([P, 2, TOPK, TOPK]),
                                  m.iota.unsqueeze(1).unsqueeze(1).to_broadcast([P, 2, TOPK, TOPK]), ALU.is_equal)\
                    .then_inc(route.sem, 1)
                own("hot")
                dve.tensor_tensor(four(hot), four(hot), three(idxf).unsqueeze(2).to_broadcast([P, 2, TOPK, TOPK]),
                                  ALU.mult).then_inc(route.sem, 1)
                own("picked")
                dve.tensor_reduce(three(pair), four(hot), AX.X, ALU.add).then_inc(route.sem, 1)
                own("pair")
                dve.scalar_tensor_tensor(out=expert[:, bass.ds(R * TOPK, TOPK)], in0=half(pair, 0), scalar=float(NKEYS),
                                         in1=half(pair, 1), op0=ALU.mult, op1=ALU.add).then_inc(route.sem, 1)
                dve.tensor_scalar(neg, best[:, 0:1], -1.0, None, ALU.mult).then_inc(route.sem, 1)
                dve.wait_ge(route_act.sem, route_act.at(R, "exp"))
                dve.reciprocal(rsum, rsum).then_inc(route.sem, 1)
                own("rsum")
                dve.tensor_scalar(gates[:, bass.ds(R * TOPK, TOPK)], ge, rsum, 0.5, ALU.mult, ALU.mult)\
                    .then_inc(route.sem, 1)

            def row_landed(G, r):
                dve.wait_ge(landed[r % RB], (G * 2 + r // RB + 1) * 16)

            def group(t, G, b, routed):
                own = lambda step: dve.wait_ge(gelu.sem, gelu.at(G, step))
                for r in range(TOPK):
                    row_landed(G, r)
                    row = ring[:, r, :]
                    dve.scalar_tensor_tensor(out=row, in0=row, scalar=1.0, in1=xm[:, t, :], op0=ALU.mult, op1=ALU.mult,
                                             accum_out=act_u[b][:, r:r + 1]).then_inc(used, 1)
                dve.wait_ge(used, G * ROWS + TOPK)
                dve.tensor_tensor(t1[b], act_u[b], act_u[b], ALU.mult).then_inc(gelu.sem, 1)
                own("sq")
                dve.tensor_scalar(t1[b], t1[b], 0.044715, 1.0, ALU.mult, ALU.add).then_inc(gelu.sem, 1)
                own("cubic")
                dve.tensor_tensor(t1[b], t1[b], act_u[b], ALU.mult).then_inc(gelu.sem, 1)
                if routed:
                    route_head(G + EH)
                dve.wait_ge(gelu_act.sem, gelu_act.at(G, "tanh"))
                dve.scalar_tensor_tensor(out=wv[b], in0=tanh[b], scalar=1.0, in1=act_u[b], op0=ALU.add, op1=ALU.mult)\
                    .then_inc(gelu.sem, 1)
                own("half")
                dve.tensor_tensor(wv[b], wv[b], gates[:, bass.ds(G * TOPK, TOPK)], ALU.mult).then_inc(gelu.sem, 1)
                own("weight")
                for r in range(TOPK):
                    row_landed(G, TOPK + r)
                    if r >= 2:
                        dve.wait_ge(used, G * ROWS + TOPK + r - 1)
                    dve.scalar_tensor_tensor(out=acc[r % 2], in0=ring[:, r, :], scalar=wv[b][:, r:r + 1], in1=acc[r % 2],
                                             op0=ALU.mult, op1=ALU.add).then_inc(used, 1)

            def tile(t, c, routed):
                for n in range(2):
                    if not is_first(t):
                        dve.wait_ge(fin.sem, fin.at(t - 1, "done"))
                    dve.memset(acc[n], 0.0).then_inc(fin.sem, 1)
                if routed:
                    prepare(t + 1, 1)
                dve.wait_ge(fin.sem, fin.at(t, "z1"))
                dve.wait_ge(prep_act.sem, prep_act.at(t, "xm"))
                dve.sem_inc(passed, 1)
                with dve.Fori(0, PAIRS) as j:
                    for b in range(2):
                        group(t, t * EH + j * 2 + b, b, routed)
                dve.wait_ge(used, (t + 1) * EH * ROWS)
                own = lambda step: dve.wait_ge(fin.sem, fin.at(t, step))
                z = acc[0]
                dve.tensor_tensor(z, z, acc[1], ALU.add).then_inc(fin.sem, 1)
                own("both")
                dve.tensor_tensor(z, z, m.mod[:, 2, c, :], ALU.mult).then_inc(fin.sem, 1)
                own("scaled")
                dve.scalar_tensor_tensor(out=z, in0=m.X[:, t, :], scalar=ALPHA, in1=z, op0=ALU.mult,
                                         op1=ALU.add).then_inc(fin.sem, 1)
                layer_norm(nc, dve, m, fin, fin_act, t, z, m.X[:, t, :], "added", passed)

            dve.wait_ge(rows_in, 16 * N_ROWS_IN)
            prepare(0, 0)
            route_head(0)
            with dve.Fori(1, EH) as R:
                route_head(R)
            tile(0, 0, True)
            with dve.Fori(1, NT - 1) as t:
                tile(t, 1, True)
            tile(NT - 1, 1, False)


def store_stream(nc, m, a):
    with Stage(nc, "store") as st:
        stored = st.sem("stored")
        block = st.block()

        @block.sync
        def _(sp):
            sp.dma_start(a["y_prompt"][0], m.X[:, 0, :]).then_inc(stored, 16)
            sp.dma_start(a["y_sample"][0].rearrange("(t p) d -> p t d", p=P), m.X[:, 1:NT, :]).then_inc(stored, 16)
            sp.wait_ge(stored, 32)


def trunk(nc, a, const_cols, where):
    a = dict(a, rows=nc.dram_tensor("modulation_rows", (LAYERS, 2, CHUNKS * D), F32).ap())
    with ExitStack() as ctx:
        m = allocate(nc, ctx, const_cols)
        view_constants(m, where)
        load_constants(nc, m, a)
        for layer in range(LAYERS):
            modulation_rows(nc, m, a, layer)
            load_modulation(nc, m, a, layer, 0, (0, 1, 2), "mix")
            modulate_transpose(nc, m, a, layer)
            project(nc, m, a, layer)
            (mlstm_scan, gla_scan)[layer](nc, m, a)
            mixer_output(nc, m, a, layer)
            peer(nc, m, a, layer)
        store_stream(nc, m, a)


_PLAIN = ["x_prompt", "x_sample", "state_mlstm_C", "state_mlstm_n", "state_mlstm_m", "state_gla_S", "ada_w", "ada_b",
          "ln_mix_g", "ln_mix_b", "ln_ffn_g", "ln_ffn_b", "mlstm_w_in", "mlstm_b_gate", "mlstm_norm_w", "mlstm_w_out",
          "gla_w_in", "gla_w_gate2", "gla_b_gate2", "gla_norm_w", "gla_w_out", "peer_w_q", "peer_u", "peer_v"]
_OUTS = {"y_prompt": (1, SEQ, D), "y_sample": (1, DEC_SEQ, D), "new_C": (1, 2, NH, DK, DV), "new_n": (1, 2, NH, DK),
         "new_m": (1, 2, NH), "new_S": (1, 2, NH, DK, DV)}


def kernel(**inputs):
    import numpy as _np
    import concourse.bacc as _bacc
    from concourse import mybir as _mybir
    from concourse.bass_utils import run_bass_kernel_spmd as _run

    host = {name: _np.asarray(inputs[name]) for name in _PLAIN}
    cond = _np.stack([_np.asarray(inputs["c_ctx"]), _np.asarray(inputs["c"])[0]], -1)
    host["c2"] = cond.reshape(KD, P, 2).transpose(1, 0, 2).reshape(P, 2 * KD)
    host["subkeysT"] = _np.asarray(inputs["peer_subkeys"]).transpose(0, 4, 1, 2, 3).reshape(LAYERS, P, EH, 2 * NKEYS)
    host["cst"], where = constants()
    nc = _bacc.Bacc("TRN2", target_bir_lowering=False, num_devices=1)
    arrays, a = {}, {}
    for name, array in host.items():
        array = _np.ascontiguousarray(array)
        arrays["in_" + name] = array
        a[name] = nc.dram_tensor("in_" + name, array.shape, _mybir.dt.from_np(array.dtype), kind="ExternalInput").ap()
    for name, shape in _OUTS.items():
        a[name] = nc.dram_tensor("out_" + name, shape, F32, kind="ExternalOutput").ap()
    trunk(nc, a, host["cst"].shape[1], where)
    r = _run(nc, [arrays], core_ids=[0])
    return tuple(r.results[0]["out_" + name] for name in _OUTS) + (None,) * 4
```

```python
from contextlib import ExitStack

import numpy as np

import concourse.bass as bass
from concourse import mybir

F32 = mybir.dt.float32
U32 = mybir.dt.uint32
ALU = mybir.AluOpType
ACT = mybir.ActivationFunctionType
AX = mybir.AxisListType

P = 128
D = 1024
KD = D // P
HALF = 512
SEQ, DEC_SEQ = 128, 512
NT = (SEQ + DEC_SEQ) // P
LAYERS = 2
CHUNKS = 6
ALPHA = (2.0 * LAYERS) ** 0.25
EPS = 1e-5
NH, DK, DV = 4, 128, 256
HV = NH * DV
NP_ = 2 * NH * DK + 2 * HV
NG = NP_ // HALF
NEG = -1.0e30
EH, TOPK, NKEYS = 8, 16, 128
GATE_NORM = 16.0
RANK = 16
TANH_SCALE = float(np.sqrt(2.0 / np.pi))
NB, BL = 4, 32
RING = TOPK


def constants():
    i, j = np.arange(P)[:, None], np.arange(P)[None, :]
    parts = {
        "ident": i == j,
        "le": i <= j, "ge": i >= j,
        "le16": (i <= j) / GATE_NORM, "ge16": (i >= j) / GATE_NORM,
        "gt16": (i > j) / GATE_NORM, "lt16": (i < j) / GATE_NORM,
        "neg_f": np.where(j <= i, 0.0, NEG), "neg_b": np.where(j >= i, 0.0, NEG),
        "last": np.broadcast_to(i == P - 1, (P, P)), "first": np.broadcast_to(i == 0, (P, P)),
        "sel": i == np.arange(NT * NH)[None, :],
        "iota": np.broadcast_to(np.arange(TOPK)[None, :], (P, TOPK)),
        "ones": np.ones((P, P)),
    }
    at, where = 0, {}
    for name, a in parts.items():
        where[name] = (at, a.shape[1])
        at += a.shape[1]
    return np.concatenate([np.asarray(a, np.float32) for a in parts.values()], 1), where


class Mem:
    pass


def allocate(nc, ctx, const_cols):
    m = Mem()

    def sb(name, shape, dt=F32):
        return ctx.enter_context(nc.sbuf_tensor(name, shape, dt))

    m.X = sb("X", [P, NT, D])
    m.mod = sb("mod", [P, 3, 2, D])
    m.lnw = sb("lnw", [P, 2, D])
    m.cst = sb("cst", [P, const_cols])
    m.big = sb("big", [P, RING * D])
    m.wrk = sb("wrk", [P, 14336])
    m.W = m.wrk[:, 0:8192].rearrange("p (s k n) -> p s k n", s=2, k=KD)
    m.hT = m.wrk[:, 8192:13312].rearrange("p (t k n) -> p t k n", t=NT, k=KD)
    m.H = m.wrk[:, 8192:13312].rearrange("p (t n) -> p t n", t=NT)
    m.y = sb("y", [P, D])
    m.yT = sb("yT", [P, KD, P])
    m.proj = m.big[:, 0:NT * NP_].rearrange("p (t n) -> p t n", t=NT)
    m.gates = sb("gates", [P, NT, 32])
    m.stat = sb("stat", [P, 64])
    m.scr = sb("scr", [P, 512])
    m.qk = sb("qk", [P, 4 * HALF])
    m.hot = sb("hot", [P, 2 * TOPK * TOPK])
    m.qhT = sb("qhT", [P, 2, 2 * P])
    m.route_gate = sb("route_gate", [P, NT * EH * TOPK])
    m.ps = ctx.enter_context(nc.psum_tensor("ps", [P, 8, HALF], F32))
    m.diag = sb("diag", [P, D])
    m.silu_c = m.diag[:, 0:32 * KD].rearrange("p (k c) -> p k c", k=KD)
    return m


class Stage:

    def __init__(self, nc, name):
        self.nc, self.name, self.sems, self.ctx = nc, name, [], ExitStack()

    def sem(self, name):
        self.sems.append(self.nc.alloc_semaphore(f"{self.name}_{name}"))
        return self.sems[-1]

    def block(self):
        return self.ctx.enter_context(self.nc.Block())

    def __enter__(self):
        return self

    def __exit__(self, *failed):
        self.ctx.__exit__(*failed)
        if failed[0] is None:
            self.nc.clear_and_free_semaphores(self.sems)
            self.nc.all_engine_barrier()


def modulation_rows(nc, m, a, layer):
    NGRP = CHUNKS * D // HALF
    w = a["ada_w"][layer].rearrange("(k p) n -> p k n", p=P)
    with Stage(nc, f"mod{layer}") as st:
        w_full = [st.sem("w_full0"), st.sem("w_full1")]
        ps_full, row_done, c_loaded, c_step, stored, stream_in, cleared, bias_in = (
            st.sem(n) for n in ("ps_full", "row_done", "c_loaded", "c_step", "stored", "stream_in", "cleared", "bias_in"))
        rows = m.big[:, 0:NGRP * P]
        bias = m.big[:, NGRP * P:2 * NGRP * P]
        cv = m.yT[:, 0, 0:2 * KD]
        ex = m.yT[:, 0, 2 * KD:4 * KD]
        cs = m.silu_c
        pairs = lambda x: x.rearrange("p (k c) -> p k c", k=KD)
        blocks = lambda row: row.rearrange("(g b n) -> b g n", b=4, n=P)
        at_blocks = lambda x, c: x[c:P:32, :].rearrange("b (g n) -> b g n", n=P)
        block = st.block()

        @block.sync
        def _(sp):
            sp.dma_start(cv, a["c2"]).then_inc(c_loaded, 16)

            def load(it, first):
                for s in range(2):
                    g = it * 2 + s
                    if not first:
                        sp.wait_ge(ps_full, g - 1)
                    sp.dma_start(m.W[:, s], w[:, :, bass.ds(g * HALF, HALF)]).then_inc(w_full[s], 16)

            load(0, True)
            sp.wait_ge(cleared, 2)
            for c in range(2):
                sp.dma_start(at_blocks(bias, c), blocks(a["ada_b"][layer])).then_inc(bias_in, 16)
            with sp.Fori(1, NGRP // 2) as it:
                load(it, False)
            sp.dma_start(m.cst[:], a["cst"]).then_inc(stream_in, 16)
            sp.dma_start(m.X[:, 0, :], a["x_prompt"][0]).then_inc(stream_in, 16)
            sp.dma_start(m.X[:, 1:NT, :], a["x_sample"][0].rearrange("(t p) d -> p t d", p=P)).then_inc(stream_in, 16)
            sp.wait_ge(row_done, NGRP)
            for c in range(2):
                sp.dma_start(blocks(a["rows"][layer, c]), at_blocks(rows, c)).then_inc(stored, 16)
            sp.wait_ge(stored, 16 * 2)
            sp.wait_ge(stream_in, 48)

        @block.tensor
        def _(pe):
            pe.wait_ge(c_step, 4)

            def products(it, first):
                for s in range(2):
                    g = it * 2 + s
                    pe.wait_ge(w_full[s], it * 16 + 16)
                    if not first:
                        pe.wait_ge(row_done, g - 1)
                    for k in range(KD):
                        for b in range(4):
                            mm = pe.matmul(m.ps[32 * b:32 * b + 32, s, 0:P], cs[:, k, :],
                                           m.W[:, s, k, b * P:(b + 1) * P], start=k == 0, stop=k == KD - 1)
                    mm.then_inc(ps_full, 1)

            products(0, True)
            with pe.Fori(1, NGRP // 2) as it:
                products(it, False)

        @block.scalar
        def _(act):
            act.wait_ge(c_loaded, 16)
            act.activation(ex, cv, ACT.Exp, scale=-1.0).then_inc(c_step, 1)

        @block.vector
        def _(dve):
            dve.memset(cs, 0.0).then_inc(cleared, 1)
            dve.memset(bias, 0.0).then_inc(cleared, 1)
            dve.wait_ge(c_step, 1)
            dve.tensor_scalar(ex, ex, 1.0, None, ALU.add).then_inc(c_step, 1)
            dve.wait_ge(c_step, 2)
            dve.reciprocal(ex, ex).then_inc(c_step, 1)
            dve.wait_ge(c_step, 3)
            dve.wait_ge(cleared, 2)
            dve.tensor_tensor(cs[:, :, 0:2], pairs(ex), pairs(cv), ALU.mult).then_inc(c_step, 1)
            dve.wait_ge(bias_in, 16 * 2)
            with dve.Fori(0, NGRP // 2) as it:
                for s in range(2):
                    g = it * 2 + s
                    dve.wait_ge(ps_full, g + 1)
                    dve.tensor_tensor(rows[:, bass.ds(g * P, P)], m.ps[:, s, 0:P],
                                      bias[:, bass.ds(g * P, P)], ALU.add).then_inc(row_done, 1)


def project(nc, m, a, layer):
    w_in = a[("mlstm_w_in", "gla_w_in")[layer]]
    G = w_in.shape[1] - NP_
    gate = (ACT.Sigmoid, ACT.Silu)[layer]
    w = w_in.rearrange("(k p) n -> p k n", p=P)
    BANKS = 5
    with Stage(nc, f"proj{layer}") as st:
        w_full = [st.sem("w_full0"), st.sem("w_full1")]
        rows_in = [st.sem("rows_in_prompt"), st.sem("rows_in_latents")]
        wg_full, ps_full, ps_read, modulated, transposed, copied = (
            st.sem(n) for n in ("wg_full", "ps_full", "ps_read", "modulated", "transposed", "copied"))
        wg = m.yT[:].rearrange("p k n -> p (k n)")[:, 0:KD * 32].rearrange("p (k g) -> p k g", k=KD)[:, :, 0:G]
        block = st.block()

        @block.sync
        def _(sp):
            for c in range(2):
                for n in (1, 0):
                    row = a["rows"][layer, c, n * D:(n + 1) * D]
                    sp.dma_start(m.mod[:, n, c, :], row.partition_broadcast(P)).then_inc(rows_in[c], 16)

            def load(it, first):
                for s in range(2):
                    if not first:
                        sp.wait_ge(ps_full, (it * 2 + s - 1) * NT)
                    sp.dma_start(m.W[:, s], w[:, :, bass.ds((it * 2 + s) * HALF, HALF)]).then_inc(w_full[s], 16)

            load(0, True)
            sp.dma_start(wg, w[:, :, NP_:NP_ + G]).then_inc(wg_full, 16)
            with sp.Fori(1, NG // 2) as it:
                load(it, False)

        @block.vector
        def _(dve):
            for t in range(NT):
                c = min(t, 1)
                if t < 2:
                    dve.wait_ge(rows_in[c], 32)
                if t > 0:
                    dve.wait_ge(transposed, t)
                dve.scalar_tensor_tensor(out=m.y[:], in0=m.mod[:, 1, c, :], scalar=1.0, in1=m.X[:, t, :], op0=ALU.add,
                                         op1=ALU.mult).then_inc(modulated, 1)
                dve.wait_ge(modulated, t * 2 + 1)
                dve.tensor_tensor(m.y[:], m.y[:], m.mod[:, 0, c, :], ALU.add).then_inc(modulated, 1)

        @block.tensor
        def _(pe):
            def transpose(t):
                pe.wait_ge(modulated, t * 2 + 2)
                if t > 0:
                    pe.wait_ge(copied, t)
                for k in range(KD):
                    tr = pe.transpose(m.ps[:, 5 + k // 4, (k % 4) * P:(k % 4 + 1) * P], m.y[:, k * P:(k + 1) * P],
                                      m.ident)
                tr.then_inc(transposed, 1)

            def products(it, first):
                for s in range(2):
                    pe.wait_ge(w_full[s], it * 16 + 16)
                    for t in range(NT):
                        u = s * NT + t
                        if first and s == 0:
                            if t < NT - 1:
                                transpose(t + 1)
                            pe.wait_ge(copied, t + 1)
                        if not first or u >= BANKS:
                            pe.wait_ge(ps_read, it * 2 * NT + u - BANKS + 1)
                        for k in range(KD):
                            mm = pe.matmul(m.ps[:, u % BANKS, :], m.hT[:, t, k, :], m.W[:, s, k, :],
                                           start=k == 0, stop=k == KD - 1)
                        mm.then_inc(ps_full, 1)

            transpose(0)
            products(0, True)
            with pe.Fori(1, NG // 2) as it:
                products(it, False)
            pe.wait_ge(wg_full, 16)
            for t in range(NT):
                for k in range(KD):
                    mm = pe.matmul(m.ps[:, 7, t * G:(t + 1) * G], m.hT[:, t, k, :], wg[:, k, :],
                                   start=k == 0, stop=k == KD - 1)
            mm.then_inc(ps_full, 1)

        @block.scalar
        def _(act):
            def read(it, func, copies=()):
                for s in range(2):
                    for t in range(NT):
                        u = s * NT + t
                        if s == 0 and t + 1 in copies:
                            copy(t + 1)
                        act.wait_ge(ps_full, it * 2 * NT + u + 1)
                        act.activation(m.proj[:, t, bass.ds((it * 2 + s) * HALF, HALF)],
                                       m.ps[:, u % BANKS, :], func).then_inc(ps_read, 1)

            def copy(t):
                act.wait_ge(transposed, t + 1)
                act.copy(m.hT[:, t, :, :].rearrange("p k n -> p (k n)"),
                         m.ps[:, 5:7, :].rearrange("p b n -> p (b n)")).then_inc(copied, 1)

            copy(0)
            read(0, ACT.Copy, range(1, NT))
            with act.Fori(1, NG // 2 - 1) as it:
                read(it, ACT.Copy)
            read(NG // 2 - 1, gate)
            act.wait_ge(ps_full, NG * NT + 1)
            act.copy(m.gates[:, :, 0:G], m.ps[:, 7, 0:NT * G].rearrange("p (t g) -> p t g", t=NT)).then_inc(ps_read, 1)


def view_constants(m, where):
    view = lambda name: m.cst[:, where[name][0]:where[name][0] + where[name][1]]
    m.ident = view("ident")
    m.le = view("le")
    m.ge = view("ge")
    m.le16 = view("le16")
    m.ge16 = view("ge16")
    m.gt16 = view("gt16")
    m.lt16 = view("lt16")
    m.neg_f = view("neg_f")
    m.neg_b = view("neg_b")
    m.last = view("last")
    m.first = view("first")
    m.sel = view("sel")
    m.iota = view("iota")
    m.ones = view("ones")


class Order:

    def __init__(self, sem, steps):
        self.sem, self.steps = sem, steps.split()

    def at(self, i, step):
        return i * len(self.steps) + self.steps.index(step) + 1


def is_first(i):
    return isinstance(i, int) and i == 0


def tiles_of(engine, i, ahead=0):
    if isinstance(i, int):
        return (i + ahead, NT - i - ahead) if i + ahead else (0, 0)
    return i + ahead, engine.snap(i * -1 + (NT - ahead))


def mlstm_scan(nc, m, a):
    FW, BW = 0, 1
    base = [m.wrk[:, 0:8192], m.mod[:].rearrange("p a c n -> p (a c n)")]
    at = [0]

    def part(n):
        at[0] += n
        return [b[:, at[0] - n:at[0]] for b in base]

    qk, qT, kT, E, ST, kw, qs, qsT = part(2 * HALF), *(part(HALF) for _ in range(7))
    C = part(NH * DV)
    small = [m.scr[:, 0:64], m.scr[:, 64:128]]
    amax, mu, mprev, blm, den, n_st = ([s[:, 4 * j:4 * j + 4] for s in small] for j in range(6))
    bm = [s[:, 24:32] for s in small]
    last = [s[:, 32:40] for s in small]
    args = [s[:, 40:56] for s in small]
    b_all = [m.scr[:, 128 + 32 * d:128 + 32 * d + NT * NH].rearrange("p (t h) -> p t h", t=NT) for d in range(2)]
    a_all = [m.scr[:, 192 + 32 * d:192 + 32 * d + NT * NH].rearrange("p (t h) -> p t h", t=NT) for d in range(2)]
    lf = [m.scr[:, 256 + 32 * d:256 + 32 * d + NT * NH] for d in range(2)]
    tmp = [m.scr[:, 320 + 32 * d:320 + 32 * d + NT * NH] for d in range(2)]
    bg = m.scr[:, 384:400]
    G = m.gates[:, :, 0:16].rearrange("p t (d k h) -> p d k t h", d=2, k=2)
    heads = lambda x: x.rearrange("p (h n) -> p h n", h=NH)
    spread = lambda x, n: x.unsqueeze(2).to_broadcast([P, NH, n])
    cumulate, neg, final = [m.le, m.ge], [m.neg_f, m.neg_b], [m.last, m.first]
    bank = lambda d, j: m.ps[:, 4 * d + j, :]
    KSCALE = DK ** -0.5
    m_out = [m.scr[:, 400 + 4 * d:404 + 4 * d] for d in range(2)]
    m_in = [m.scr[:, 408 + 4 * d:412 + 4 * d] for d in range(2)]

    with Stage(nc, "mlstm") as st:
        pool_, dve_, act_, pe_ = ([Order(st.sem(f"{e}_done{d}"), s) for d in range(2)] for e, s in (
            ("pool", "qk"),
            ("dve", "masked amax mu shifted a_ei b_t m_t a_m last blm a_wk a_dec m_new qs kw S neg_den den r "
                    "h0 h1 h2 h3 C0 C1 C2 C3 n_dec n_new"),
            ("act", "qT kT E exps ST qsT"),
            ("pe", "tq tk QK last tS tqs num den dC dn")))
        ahead_dve, ahead_pe = ([Order(st.sem(f"ahead_{e}{d}"), s) for d in range(2)] for e, s in (
            ("dve", "diag"), ("pe", "rows")))
        pre, cleared, stored, state_in, gate_in, m_swapped = (
            st.sem(n) for n in ("pre", "cleared", "stored", "state_in", "gate_in", "m_swapped"))
        block = st.block()

        @block.sync
        def _(sp):
            sp.dma_start(bg, a["mlstm_b_gate"].partition_broadcast(P)).then_inc(gate_in, 16)
            for d in range(2):
                sp.dma_start(m_in[d], a["state_mlstm_m"][0, d].partition_broadcast(P)).then_inc(gate_in, 16)
            sp.wait_ge(m_swapped, 4)
            with nc.allow_non_contiguous_dma(reason="normaliser rows of 4 bytes"):
                for d in range(2):
                    sp.wait_ge(dve_[d].sem, dve_[d].at(0, "n_new"))
                    sp.dma_start(a["new_C"][0, d].rearrange("h k v -> k h v"), heads(C[d])).then_inc(stored, 16)
                    sp.dma_start(a["new_n"][0, d].rearrange("h k -> k h"), n_st[d]).then_inc(stored, 16)
                    sp.dma_start(a["new_m"][0, d:d + 1], m_out[d][0:1, :]).then_inc(stored, 16)
                sp.wait_ge(stored, 96)
                for d in range(2):
                    sp.dma_start(heads(C[d]), a["state_mlstm_C"][0, d].rearrange("h k v -> k h v")).then_inc(state_in, 16)
                    sp.dma_start(n_st[d], a["state_mlstm_n"][0, d].rearrange("h k -> k h")).then_inc(state_in, 16)

        @block.gpsimd
        def _(pool):
            def round_(i):
                for d, t in enumerate(tiles_of(pool, i)):
                    if not isinstance(i, int):
                        pool.wait_ge(pe_[d].sem, pe_[d].at(i - 1, "tk"))
                    pool.tensor_copy(qk[d], m.proj[:, t, 0:2 * HALF]).then_inc(pool_[d].sem, 1)

            round_(0)
            for d in range(2):
                pool.memset(mprev[d], 0.0).then_inc(cleared, 1)
                pool.memset(C[d], 0.0).then_inc(cleared, 1)
                pool.memset(n_st[d], 0.0).then_inc(cleared, 1)
            pool.memset(m.H, 0.0).then_inc(cleared, 1)
            with pool.Fori(1, NT) as i:
                round_(i)

        @block.scalar
        def _(act):
            act.wait_ge(pre, 1)
            for d in range(2):
                act.activation(tmp[d].rearrange("p (t h) -> p t h", t=NT), G[:, d, 1], ACT.Abs).then_inc(pre, 1)
            act.wait_ge(pre, 3)
            for d in range(2):
                act.activation(tmp[d], tmp[d], ACT.Exp, scale=-1.0).then_inc(pre, 1)
            act.wait_ge(pre, 5)
            for d in range(2):
                act.activation(tmp[d], tmp[d], ACT.Ln, bias=1.0).then_inc(pre, 1)

            def round_(i):
                for d in range(2):
                    act.wait_ge(pe_[d].sem, pe_[d].at(i, "tq"))
                    act.copy(qT[d], bank(d, 0)).then_inc(act_[d].sem, 1)
                for d in range(2):
                    act.wait_ge(pe_[d].sem, pe_[d].at(i, "tk"))
                    act.mul(kT[d], bank(d, 1), KSCALE).then_inc(act_[d].sem, 1)
                for d in range(2):
                    act.wait_ge(dve_[d].sem, dve_[d].at(i, "shifted"))
                    act.activation(E[d], E[d], ACT.Exp).then_inc(act_[d].sem, 1)
                for d in range(2):
                    act.wait_ge(dve_[d].sem, dve_[d].at(i, "a_dec"))
                    act.activation(args[d], args[d], ACT.Exp).then_inc(act_[d].sem, 1)
                for d in range(2):
                    act.wait_ge(pe_[d].sem, pe_[d].at(i, "tS"))
                    act.copy(ST[d], bank(d, 0)).then_inc(act_[d].sem, 1)
                for d in range(2):
                    act.wait_ge(pe_[d].sem, pe_[d].at(i, "tqs"))
                    act.copy(qsT[d], bank(d, 1)).then_inc(act_[d].sem, 1)

            round_(0)
            with act.Fori(1, NT) as i:
                round_(i)

        @block.tensor
        def _(pe):
            pe.wait_ge(pre, 9)
            for d in range(2):
                mm = pe.matmul(m.ps[:, 0, d * NT * NH:(d + 1) * NT * NH], cumulate[d], lf[d], start=True, stop=True)
                mm.then_inc(pre, 1)

            def rows(i):
                for d in range(2):
                    pe.wait_ge(ahead_dve[d].sem, ahead_dve[d].at(i, "diag"))
                    pe.matmul(bank(d, 3), m.ones, ST[d], start=True, stop=True).then_inc(ahead_pe[d].sem, 1)

            def round_(i, at_end=False):
                first = is_first(i)
                tiles = tiles_of(pe, i)
                for d in range(2):
                    pe.wait_ge(pool_[d].sem, pool_[d].at(i, "qk"))
                    if first:
                        pe.wait_ge(pre, 15)
                    else:
                        pe.wait_ge(dve_[d].sem, dve_[d].at(i - 1, "C3"))
                    for n in range(2):
                        for h in range(NH):
                            tr = pe.transpose(bank(d, n)[:, h * P:(h + 1) * P],
                                              qk[d][:, n * HALF + h * P:n * HALF + (h + 1) * P], m.ident)
                        tr.then_inc(pe_[d].sem, 1)
                for d in range(2):
                    pe.wait_ge(act_[d].sem, act_[d].at(i, "kT"))
                    pe.wait_ge(dve_[d].sem, dve_[d].at(i, "masked"))
                    for h in range(NH):
                        mm = pe.matmul(bank(d, 3)[:, h * P:(h + 1) * P], qT[d][:, h * P:(h + 1) * P],
                                       kT[d][:, h * P:(h + 1) * P], start=True, stop=True)
                    mm.then_inc(pe_[d].sem, 1)
                for d in range(2):
                    pe.wait_ge(dve_[d].sem, dve_[d].at(i, "m_t"))
                    pe.matmul(bank(d, 2)[:, 0:8], final[d], bm[d], start=True, stop=True).then_inc(pe_[d].sem, 1)
                for d in range(2):
                    pe.wait_ge(dve_[d].sem, dve_[d].at(i, "S"))
                    for h in range(NH):
                        tr = pe.transpose(bank(d, 0)[:, h * P:(h + 1) * P], E[d][:, h * P:(h + 1) * P], m.ident)
                    tr.then_inc(pe_[d].sem, 1)
                    for h in range(NH):
                        tr = pe.transpose(bank(d, 1)[:, h * P:(h + 1) * P], qs[d][:, h * P:(h + 1) * P], m.ident)
                    tr.then_inc(pe_[d].sem, 1)
                if not first:
                    pe.wait_ge(state_in, 64)
                for d, t in enumerate(tiles):
                    pe.wait_ge(act_[d].sem, act_[d].at(i, "qsT"))
                    for h in range(NH):
                        out = bank(d, 2 + h // 2)[:, (h % 2) * DV:(h % 2 + 1) * DV]
                        pe.matmul(out, ST[d][:, h * P:(h + 1) * P],
                                  m.proj[:, t, 2 * HALF + h * DV:2 * HALF + (h + 1) * DV], start=True, stop=False)
                        mm = pe.matmul(out, qsT[d][:, h * P:(h + 1) * P], C[d][:, h * DV:(h + 1) * DV], start=False, stop=True)
                    mm.then_inc(pe_[d].sem, 1)
                    for h in range(NH):
                        pe.matmul(bank(d, 0)[:, h:h + 1], ST[d][:, h * P:(h + 1) * P], m.ones[:, 0:1], start=True, stop=False)
                        mm = pe.matmul(bank(d, 0)[:, h:h + 1], qsT[d][:, h * P:(h + 1) * P], n_st[d][:, h:h + 1],
                                       start=False, stop=True)
                    mm.then_inc(pe_[d].sem, 1)
                for d, t in enumerate(tiles):
                    pe.wait_ge(dve_[d].sem, dve_[d].at(i, "den"))
                    for h in range(NH):
                        mm = pe.matmul(bank(d, h // 2)[:, (h % 2) * DV:(h % 2 + 1) * DV], kw[d][:, h * P:(h + 1) * P],
                                       m.proj[:, t, 2 * HALF + h * DV:2 * HALF + (h + 1) * DV], start=True, stop=True)
                    mm.then_inc(pe_[d].sem, 1)
                for d in range(2):
                    pe.wait_ge(dve_[d].sem, dve_[d].at(i, "h3"))
                    for h in range(NH):
                        mm = pe.matmul(bank(d, 2)[:, h:h + 1], kw[d][:, h * P:(h + 1) * P], m.ones[:, 0:1],
                                       start=True, stop=True)
                    mm.then_inc(pe_[d].sem, 1)
                if not at_end:
                    rows(i + 1)

            rows(0)
            round_(0)
            with pe.Fori(1, NT - 1) as i:
                round_(i)
            round_(NT - 1, at_end=True)

        @block.vector
        def _(dve):
            dve.wait_ge(gate_in, 48)
            dve.tensor_tensor(m.gates[:, :, 0:16], m.gates[:, :, 0:16], bg.unsqueeze(1).to_broadcast([P, NT, 16]),
                              ALU.add).then_inc(pre, 1)
            dve.wait_ge(pre, 7)
            for d in range(2):
                dve.scalar_tensor_tensor(out=lf[d].rearrange("p (t h) -> p t h", t=NT), in0=G[:, d, 1], scalar=0.0,
                                         in1=tmp[d].rearrange("p (t h) -> p t h", t=NT),
                                         op0=ALU.min, op1=ALU.subtract).then_inc(pre, 1)
            dve.wait_ge(pre, 11)
            for d in range(2):
                dve.tensor_copy(b_all[d].rearrange("p t h -> p (t h)"),
                                m.ps[:, 0, d * NT * NH:(d + 1) * NT * NH]).then_inc(pre, 1)
            dve.wait_ge(pre, 13)
            for d in range(2):
                dve.tensor_tensor(a_all[d], G[:, d, 0], b_all[d], ALU.subtract).then_inc(pre, 1)
            dve.wait_ge(pre, 15)

            def diagonals(i, tiles):
                for d, t in enumerate(tiles):
                    dve.tensor_tensor(heads(ST[d]), m.ident.unsqueeze(1).to_broadcast([P, NH, P]),
                                      spread(a_all[d][:, t, :], P), ALU.mult).then_inc(ahead_dve[d].sem, 1)

            def round_(i, at_end=False):
                first = is_first(i)
                tiles = tiles_of(dve, i)

                def own(d, step):
                    dve.wait_ge(dve_[d].sem, dve_[d].at(i, step))

                for d in range(2):
                    dve.wait_ge(ahead_pe[d].sem, ahead_pe[d].at(i, "rows"))
                    dve.tensor_tensor(heads(E[d]), heads(bank(d, 3)), neg[d].unsqueeze(1).to_broadcast([P, NH, P]),
                                      ALU.add).then_inc(dve_[d].sem, 1)
                for d in range(2):
                    own(d, "masked")
                    dve.tensor_reduce(amax[d], heads(E[d]), AX.X, ALU.max).then_inc(dve_[d].sem, 1)
                for d in range(2):
                    own(d, "amax")
                    if first:
                        dve.wait_ge(cleared, 7)
                    else:
                        dve.wait_ge(m_swapped, 4)
                    dve.tensor_tensor(mu[d], amax[d], mprev[d], ALU.max).then_inc(dve_[d].sem, 1)
                for d, t in enumerate(tiles):
                    own(d, "mu")
                    dve.tensor_tensor(heads(E[d]), heads(E[d]), spread(mu[d], P), ALU.subtract).then_inc(dve_[d].sem, 1)
                    dve.tensor_tensor(args[d][:, 0:4], mprev[d], mu[d], ALU.subtract).then_inc(dve_[d].sem, 1)
                    dve.tensor_copy(bm[d][:, 0:4], b_all[d][:, t, :]).then_inc(dve_[d].sem, 1)
                    dve.tensor_tensor(bm[d][:, 4:8], b_all[d][:, t, :], mu[d], ALU.add).then_inc(dve_[d].sem, 1)
                for d in range(2):
                    own(d, "m_t")
                    dve.tensor_scalar(args[d][:, 4:8], bm[d][:, 4:8], -1.0, None, ALU.mult).then_inc(dve_[d].sem, 1)
                for d in range(2):
                    dve.wait_ge(pe_[d].sem, pe_[d].at(i, "last"))
                    dve.tensor_copy(last[d], bank(d, 2)[:, 0:8]).then_inc(dve_[d].sem, 1)
                for d in range(2):
                    own(d, "last")
                    dve.tensor_tensor(blm[d], last[d][:, 0:4], last[d][:, 4:8], ALU.subtract).then_inc(dve_[d].sem, 1)
                for d, t in enumerate(tiles):
                    own(d, "blm")
                    dve.tensor_tensor(args[d][:, 8:12], a_all[d][:, t, :], blm[d], ALU.add).then_inc(dve_[d].sem, 1)
                    dve.tensor_tensor(args[d][:, 12:16], mprev[d], blm[d], ALU.add).then_inc(dve_[d].sem, 1)
                for d in range(2):
                    own(d, "a_dec")
                    dve.tensor_copy(mprev[d], last[d][:, 4:8]).then_inc(dve_[d].sem, 1)
                for d, t in enumerate(tiles):
                    dve.wait_ge(act_[d].sem, act_[d].at(i, "exps"))
                    dve.tensor_tensor(heads(qs[d]), heads(m.proj[:, t, 0:HALF]), spread(args[d][:, 0:4], P),
                                      ALU.mult).then_inc(dve_[d].sem, 1)
                    dve.scalar_tensor_tensor(out=heads(kw[d]), in0=heads(m.proj[:, t, HALF:2 * HALF]), scalar=KSCALE,
                                             in1=spread(args[d][:, 8:12], P), op0=ALU.mult, op1=ALU.mult)\
                        .then_inc(dve_[d].sem, 1)
                for d in range(2):
                    dve.wait_ge(pe_[d].sem, pe_[d].at(i, "QK"))
                    dve.wait_ge(act_[d].sem, act_[d].at(i, "E"))
                    dve.tensor_tensor(E[d], bank(d, 3), E[d], ALU.mult).then_inc(dve_[d].sem, 1)
                for d in range(2):
                    dve.wait_ge(pe_[d].sem, pe_[d].at(i, "den"))
                    dve.scalar_tensor_tensor(out=den[d], in0=bank(d, 0)[:, 0:4], scalar=-1.0, in1=args[d][:, 4:8],
                                             op0=ALU.mult, op1=ALU.max).then_inc(dve_[d].sem, 1)
                for d in range(2):
                    own(d, "neg_den")
                    dve.tensor_tensor(den[d], bank(d, 0)[:, 0:4], den[d], ALU.max).then_inc(dve_[d].sem, 1)
                for d in range(2):
                    own(d, "den")
                    dve.reciprocal(den[d], den[d]).then_inc(dve_[d].sem, 1)
                if not at_end:
                    diagonals(i + 1, tiles_of(dve, i, 1))
                for d, t in enumerate(tiles):
                    own(d, "r")
                    if first and d == 1:
                        dve.wait_ge(dve_[0].sem, dve_[0].at(i, "h3"))
                    for h in range(NH):
                        out = m.H[:, t, h * DV:(h + 1) * DV]
                        dve.scalar_tensor_tensor(out=out, in0=bank(d, 2 + h // 2)[:, (h % 2) * DV:(h % 2 + 1) * DV],
                                                 scalar=den[d][:, h:h + 1], in1=out, op0=ALU.mult, op1=ALU.add)\
                            .then_inc(dve_[d].sem, 1)
                if not first:
                    dve.wait_ge(state_in, 64)
                for d in range(2):
                    dve.wait_ge(pe_[d].sem, pe_[d].at(i, "dC"))
                    for h in range(NH):
                        state = C[d][:, h * DV:(h + 1) * DV]
                        dve.scalar_tensor_tensor(out=state, in0=state, scalar=args[d][:, 12 + h:13 + h],
                                                 in1=bank(d, h // 2)[:, (h % 2) * DV:(h % 2 + 1) * DV],
                                                 op0=ALU.mult, op1=ALU.add).then_inc(dve_[d].sem, 1)
                    dve.tensor_tensor(n_st[d], n_st[d], args[d][:, 12:16], ALU.mult).then_inc(dve_[d].sem, 1)
                for d in range(2):
                    own(d, "n_dec")
                    dve.wait_ge(pe_[d].sem, pe_[d].at(i, "dn"))
                    dve.tensor_tensor(n_st[d], n_st[d], bank(d, 2)[:, 0:4], ALU.add).then_inc(dve_[d].sem, 1)

            diagonals(0, (0, 0))
            round_(0)
            for d in range(2):
                dve.tensor_copy(m_out[d], mprev[d]).then_inc(m_swapped, 1)
            dve.wait_ge(m_swapped, 2)
            for d in range(2):
                dve.tensor_copy(mprev[d], m_in[d]).then_inc(m_swapped, 1)
            with dve.Fori(1, NT - 1) as i:
                round_(i)
            round_(NT - 1, at_end=True)


NORM = "st0 st1 mv eps rstd centred gained"


def layer_norm(nc, dve, m, order, act_order, i, y, out, ready, passed):
    stats, mv, rs = m.stat[:, 0:12], m.stat[:, 12:14], m.stat[:, 14:15]
    own = lambda step: dve.wait_ge(order.sem, order.at(i, step))
    own(ready)
    for h in range(2):
        dve.bn_stats(stats[:, 6 * h:6 * h + 6], y[:, h * HALF:(h + 1) * HALF]).then_inc(order.sem, 1)
    own("st1")
    dve.sem_inc(passed, 1)
    dve.bn_aggr(mv, stats).then_inc(order.sem, 1)
    own("mv")
    dve.tensor_scalar(rs, mv[:, 1:2], EPS, None, ALU.add).then_inc(order.sem, 1)
    dve.wait_ge(act_order.sem, act_order.at(i, "sqrt"))
    dve.reciprocal(rs, rs).then_inc(order.sem, 1)
    own("rstd")
    dve.tensor_scalar(y, y, mv[:, 0:1], rs, ALU.subtract, ALU.mult).then_inc(order.sem, 1)
    own("centred")
    dve.tensor_tensor(y, y, m.lnw[:, 0, :], ALU.mult).then_inc(order.sem, 1)
    own("gained")
    dve.tensor_tensor(out, y, m.lnw[:, 1, :], ALU.add).then_inc(order.sem, 1)


def layer_norm_sqrt(act, m, order, act_order, i):
    act.wait_ge(order.sem, order.at(i, "eps"))
    act.activation(m.stat[:, 14:15], m.stat[:, 14:15], ACT.Sqrt).then_inc(act_order.sem, 1)


def mixer_output(nc, m, a, layer):
    w = a[("mlstm_w_out", "gla_w_out")[layer]].rearrange("(k p) n -> p k n", p=P)
    norm_w = a[("mlstm_norm_w", "gla_norm_w")[layer]]
    W = m.wrk[:, 0:KD * D].rearrange("p (k n) -> p k n", k=KD)
    nw = m.qk[:, 0:D]
    z = m.big[:, NT * NP_:NT * NP_ + D]
    st6 = m.stat[:, 16:40]
    mv = m.scr[:, 0:8].rearrange("p (h s) -> p h s", h=NH)
    var = m.scr[:, 8:12]
    more = layer + 1 < LAYERS
    SLOTS, PER_TILE, WIDTH = 3, 6, 2 * P
    NB4 = WIDTH // 4
    NGRP = CHUNKS * D // WIDTH
    assert NGRP == PER_TILE * (NT - 1)
    ada = a["ada_w"][min(layer + 1, LAYERS - 1)].rearrange("(k p) n -> p k n", p=P)
    slot = [m.proj[:, s, 0:KD * WIDTH].rearrange("p (k n) -> p k n", k=KD) for s in range(SLOTS)]
    rows, bias = (m.proj[:, SLOTS + n, 0:NGRP * NB4] for n in range(2))
    blocks = lambda row: row.rearrange("(g b n) -> b g n", b=4, n=NB4)
    at_blocks = lambda x, c: x[c:P:32, :].rearrange("b (g n) -> b g n", n=NB4)
    row_ps = lambda q: m.ps[:, 4 + q // 2, (q % 2) * NB4:(q % 2 + 1) * NB4]
    with Stage(nc, f"out{layer}") as st:
        head = Order(st.sem("head"), "b0 b1 b2 b3 a0 a1 a2 a3 sq ms eps rstd n0 n1 n2 n3 weighed gated")
        rest = Order(st.sem("rest"), "scaled added " + NORM + " done")
        head_act, rest_act = Order(st.sem("head_act"), "sqrt"), Order(st.sem("rest_act"), "sqrt")
        loaded, transposed, copied, product = (st.sem(n) for n in ("loaded", "transposed", "copied", "product"))
        passed, norm_loaded, next_in = (st.sem(n) for n in ("passed", "norm_loaded", "next_in"))
        w_loaded = [st.sem("w_loaded0"), st.sem("w_loaded1")]
        slot_full = [st.sem(f"slot_full{s}") for s in range(SLOTS)]
        cleared, bias_in, row_full, row_done, stored = (
            st.sem(n) for n in ("cleared", "bias_in", "row_full", "row_done", "stored"))
        block = st.block()

        @block.sync
        def _(sp):
            for h in range(HV // norm_w.shape[0]):
                s = norm_w.shape[0]
                sp.dma_start(nw[:, h * s:(h + 1) * s], norm_w.partition_broadcast(P)).then_inc(norm_loaded, 16)
            sp.dma_start(W[:, :, 0:HALF], w[:, :, 0:HALF]).then_inc(w_loaded[0], 16)
            load_rows(sp, m, a, layer, 0, (2,), "mix", loaded)
            sp.dma_start(W[:, :, HALF:D], w[:, :, HALF:D]).then_inc(w_loaded[1], 16)
            for n in (1, 0):
                for c in range(2):
                    row = a["rows"][layer, c, (3 + n) * D:(4 + n) * D]
                    sp.dma_start(m.mod[:, n, c, :], row.partition_broadcast(P)).then_inc(next_in, 16)
            if more:
                def load(n):
                    for s in range(SLOTS):
                        g = n * SLOTS + s
                        if not is_first(n):
                            sp.wait_ge(row_full, g - SLOTS + 1)
                        sp.dma_start(slot[s], ada[:, :, bass.ds(g * WIDTH, WIDTH)]).then_inc(slot_full[s], 16)

                load(0)
                sp.wait_ge(cleared, 1)
                for c in range(2):
                    sp.dma_start(at_blocks(bias, c), blocks(a["ada_b"][layer + 1])).then_inc(bias_in, 16)
                with sp.Fori(1, NGRP // SLOTS) as n:
                    load(n)
                sp.wait_ge(row_done, NGRP // 2)
                for c in range(2):
                    sp.dma_start(blocks(a["rows"][layer + 1, c]), at_blocks(rows, c)).then_inc(stored, 16)
                sp.wait_ge(stored, 16 * 2)
            sp.wait_ge(next_in, 64)

        if more:
            @block.gpsimd
            def _(pool):
                pool.memset(bias, 0.0).then_inc(cleared, 1)

        n_norm = HV // norm_w.shape[0]

        @block.tensor
        def _(pe):
            def tile(t, rows_too):
                first = is_first(t)
                pe.wait_ge(head.sem, head.at(t, "gated"))
                if not first:
                    pe.wait_ge(copied, t)
                for k in range(KD):
                    tr = pe.transpose(m.ps[:, k // 4, (k % 4) * P:(k % 4 + 1) * P], m.y[:, k * P:(k + 1) * P], m.ident)
                tr.then_inc(transposed, 1)
                if not first:
                    pe.wait_ge(rest.sem, rest.at(t - 1, "scaled"))
                pe.wait_ge(copied, t + 1)
                for n in range(2):
                    if first:
                        pe.wait_ge(w_loaded[n], 16)
                    for k in range(KD):
                        mm = pe.matmul(m.ps[:, 2 + n, :], m.yT[:, k, :], W[:, k, n * HALF:(n + 1) * HALF],
                                       start=k == 0, stop=k == KD - 1)
                    if n == 1:
                        mm.then_inc(product, 1)
                    if rows_too:
                        row_groups(t, n * PER_TILE // 2)

            def row_groups(t, start):
                for q in range(start, start + PER_TILE // 2):
                    pe.wait_ge(slot_full[q % SLOTS], ((t - 1) * (PER_TILE // SLOTS) + q // SLOTS + 1) * 16)
                    if not isinstance(t, int):
                        pe.wait_ge(row_done, (t - 2) * (PER_TILE // 2) + q // 2 + 1)
                    for k in range(KD):
                        for b in range(4):
                            mm = pe.matmul(row_ps(q)[32 * b:32 * b + 32, :], m.silu_c[:, k, :],
                                           slot[q % SLOTS][:, k, b * NB4:(b + 1) * NB4], start=k == 0, stop=k == KD - 1)
                    mm.then_inc(row_full, 1)

            tile(0, False)
            if more:
                tile(1, True)
            with pe.Fori(2 if more else 1, NT) as t:
                tile(t, more)

        @block.scalar
        def _(act):
            def sqrt_head(t):
                act.wait_ge(head.sem, head.at(t, "eps"))
                act.activation(var, var, ACT.Sqrt).then_inc(head_act.sem, 1)

            def evacuate(t):
                act.wait_ge(transposed, t + 1)
                if not is_first(t):
                    act.wait_ge(product, t)
                act.copy(m.yT[:].rearrange("p k n -> p (k n)"), m.ps[:, 0:2, :].rearrange("p b n -> p (b n)"))\
                    .then_inc(copied, 1)

            sqrt_head(0)
            evacuate(0)
            with act.Fori(1, NT) as t:
                sqrt_head(t)
                evacuate(t)
                layer_norm_sqrt(act, m, rest, rest_act, t - 1)
            layer_norm_sqrt(act, m, rest, rest_act, NT - 1)

        @block.vector
        def _(dve):
            def head_norm(t):
                own = lambda step: dve.wait_ge(head.sem, head.at(t, step))
                hh = lambda h: m.H[:, t, h * DV:(h + 1) * DV]
                for h in range(NH):
                    dve.bn_stats(st6[:, 6 * h:6 * h + 6], hh(h)).then_inc(head.sem, 1)
                own("b3")
                dve.sem_inc(passed, 1)
                for h in range(NH):
                    dve.bn_aggr(mv[:, h, :], st6[:, 6 * h:6 * h + 6]).then_inc(head.sem, 1)
                own("a3")
                dve.tensor_tensor(var, mv[:, :, 0], mv[:, :, 0], ALU.mult).then_inc(head.sem, 1)
                own("sq")
                dve.scalar_tensor_tensor(out=var, in0=var, scalar=float(layer == 1), in1=mv[:, :, 1], op0=ALU.mult,
                                         op1=ALU.add).then_inc(head.sem, 1)
                own("ms")
                dve.tensor_scalar(var, var, EPS, None, ALU.add).then_inc(head.sem, 1)
                dve.wait_ge(head_act.sem, head_act.at(t, "sqrt"))
                dve.reciprocal(var, var).then_inc(head.sem, 1)
                own("rstd")
                if not is_first(t):
                    dve.wait_ge(transposed, t)
                for h in range(NH):
                    y = m.y[:, h * DV:(h + 1) * DV]
                    if layer == 0:
                        ins = dve.tensor_scalar(y, hh(h), mv[:, h, 0:1], var[:, h:h + 1], ALU.subtract, ALU.mult)
                    else:
                        ins = dve.tensor_scalar(y, hh(h), var[:, h:h + 1], None, ALU.mult)
                    ins.then_inc(head.sem, 1)
                own("n3")
                if is_first(t):
                    dve.wait_ge(norm_loaded, 16 * n_norm)
                dve.tensor_tensor(m.y[:], m.y[:], nw, ALU.mult).then_inc(head.sem, 1)
                own("weighed")
                dve.tensor_tensor(m.y[:], m.y[:], m.proj[:, t, 4 * HALF:6 * HALF], ALU.mult).then_inc(head.sem, 1)

            def residual(t, c):
                dve.wait_ge(product, t + 1)
                if not is_first(t):
                    dve.wait_ge(rest.sem, rest.at(t - 1, "done"))
                dve.tensor_tensor(z, m.ps[:, 2:4, :].rearrange("p b n -> p (b n)"), m.mod[:, 2, c, :],
                                  ALU.mult).then_inc(rest.sem, 1)
                dve.wait_ge(rest.sem, rest.at(t, "scaled"))
                dve.scalar_tensor_tensor(out=z, in0=m.X[:, t, :], scalar=ALPHA, in1=z, op0=ALU.mult,
                                         op1=ALU.add).then_inc(rest.sem, 1)
                layer_norm(nc, dve, m, rest, rest_act, t, z, m.X[:, t, :], "added", passed)

            def row_groups(t):
                for q in range(0, PER_TILE, 2):
                    g = (t - 1) * PER_TILE + q
                    dve.wait_ge(row_full, g + 2)
                    dve.tensor_tensor(rows[:, bass.ds(g * NB4, 2 * NB4)], m.ps[:, 4 + q // 2, 0:2 * NB4],
                                      bias[:, bass.ds(g * NB4, 2 * NB4)], ALU.add).then_inc(row_done, 1)

            head_norm(0)
            head_norm(1)
            dve.wait_ge(loaded, 16 * 4)
            residual(0, 0)
            if more:
                dve.wait_ge(bias_in, 16 * 2)
            with dve.Fori(2, NT) as t:
                head_norm(t)
                residual(t - 1, 1)
                if more:
                    row_groups(t - 1)
            residual(NT - 1, 1)
            if more:
                row_groups(NT - 1)


def load_rows(sp, m, a, layer, first, which, ln, sem):
    for n in which:
        for c in range(2):
            row = a["rows"][layer, c, (first + n) * D:(first + n + 1) * D]
            sp.dma_start(m.mod[:, n, c, :], row.partition_broadcast(P)).then_inc(sem, 16)
    for n, name in enumerate(("g", "b")):
        sp.dma_start(m.lnw[:, n, :], a[f"ln_{ln}_{name}"][layer].partition_broadcast(P)).then_inc(sem, 16)


def gla_scan(nc, m, a):
    base = [m.wrk[:, 0:8192], m.mod[:].rearrange("p a c n -> p (a c n)")]
    at = [0]

    def part(n):
        at[0] += n
        return [b[:, at[0] - n:at[0]] for b in base]

    KB = part(NB * HALF)
    qT, kT, la, bcS, full, ql, kl, A = (part(HALF) for _ in range(8))
    AT = qT
    S = [m.wrk[:, 7168:8192], m.wrk[:, 13312:14336]]
    x = [m.hot[:], m.qhT[:].rearrange("p a n -> p (a n)")]
    g16 = [m.scr[:, 16 * d:16 * d + 16] for d in range(2)]
    decay = [m.scr[:, 32 + 4 * d:36 + 4 * d] for d in range(2)]
    gT = [m.y[0:RANK, P * d:P * (d + 1)] for d in range(2)]
    w2 = [m.yT[:].rearrange("p k n -> p (k n)")[0:RANK, HALF * d:HALF * (d + 1)] for d in range(2)]
    bg = [m.big[:, NT * NP_ + HALF * d:NT * NP_ + HALF * (d + 1)] for d in range(2)]
    qk = [m.qk[:, 0:2 * HALF], m.qk[:, 2 * HALF:4 * HALF]]
    heads = lambda v: v.rearrange("p (h n) -> p h n", h=NH)
    blocks = lambda v: v.rearrange("p (h b n) -> p h b n", h=NH, b=NB)
    cumulate, rest16, causal = [m.le16, m.ge16], [m.gt16, m.lt16], [m.ge, m.le]
    final = [P - 1, 0]
    bank = lambda d, j: m.ps[:, 4 * d + j, :]
    QSCALE = DK ** -0.5

    def keys(d, i):
        return slice(0, BL * (i + 1)) if d == 0 else slice(BL * i, P)

    def before(d, i):
        t = BL * i - 1 if d == 0 else BL * (i + 1)
        return t if 0 <= t < P else None

    def start_block(d):
        return 0 if d == 0 else NB - 1

    with Stage(nc, "gla") as st:
        pool_, dve_, act_, pe_ = ([Order(st.sem(f"{e}_done{d}"), s) for d in range(2)] for e, s in (
            ("pool", "qk"),
            ("dve", "ql0 ql kb0 kb1 kb2 kb3 decay qd qf kl keys0 keys1 keys2 keys3 A o S0 S1 S2 S3"),
            ("act", "qT kT bcS full kl ql kb0 kb1 kb2 kb3 AT"),
            ("pe", "tq tk bc suffix A tA o dS")))
        gate_dve, gate_act, gate_pe = ([Order(st.sem(f"gate_{e}{d}"), s) for d in range(2)] for e, s in (
            ("dve", "g16 x la"), ("act", "gT abs exp ln"), ("pe", "tg gates")))
        cleared, stored, state_in, loaded = (st.sem(n) for n in ("cleared", "stored", "state_in", "loaded"))
        block = st.block()

        @block.sync
        def _(sp):
            for d in range(2):
                sp.dma_start(w2[d], a["gla_w_gate2"][d]).then_inc(loaded, 16)
                sp.dma_start(bg[d], a["gla_b_gate2"][d].partition_broadcast(P)).then_inc(loaded, 16)
            for d in range(2):
                sp.wait_ge(dve_[d].sem, dve_[d].at(0, "S3"))
                sp.dma_start(a["new_S"][0, d].rearrange("h k v -> k h v"), heads(S[d])).then_inc(stored, 16)
            sp.wait_ge(stored, 32)
            for d in range(2):
                sp.dma_start(heads(S[d]), a["state_gla_S"][0, d].rearrange("h k v -> k h v")).then_inc(state_in, 16)

        @block.gpsimd
        def _(pool):
            def round_(i):
                for d, t in enumerate(tiles_of(pool, i)):
                    if not is_first(i):
                        pool.wait_ge(pe_[d].sem, pe_[d].at(i - 1, "tk"))
                    pool.tensor_copy(qk[d], m.proj[:, t, 0:2 * HALF]).then_inc(pool_[d].sem, 1)

            round_(0)
            for d in range(2):
                pool.memset(KB[d], 0.0).then_inc(cleared, 1)
                pool.memset(S[d], 0.0).then_inc(cleared, 1)
            pool.memset(m.H, 0.0).then_inc(cleared, 1)
            with pool.Fori(1, NT) as i:
                round_(i)

        @block.scalar
        def _(act):
            def round_(i):
                def after_pe(d, step):
                    act.wait_ge(pe_[d].sem, pe_[d].at(i, step))

                for d in range(2):
                    after_pe(d, "tq")
                    if not is_first(i):
                        act.wait_ge(dve_[d].sem, dve_[d].at(i - 1, "keys3"))
                    act.mul(qT[d], bank(d, 0), QSCALE).then_inc(act_[d].sem, 1)
                    after_pe(d, "tk")
                    act.copy(kT[d], bank(d, 1)).then_inc(act_[d].sem, 1)
                for d in range(2):
                    after_pe(d, "bc")
                    act.copy(bcS[d], bank(d, 2)).then_inc(act_[d].sem, 1)
                    act.activation(full[d], bank(d, 2), ACT.Exp).then_inc(act_[d].sem, 1)
                    after_pe(d, "suffix")
                    act.activation(kl[d], bank(d, 3), ACT.Exp).then_inc(act_[d].sem, 1)
                for d in range(2):
                    act.wait_ge(dve_[d].sem, dve_[d].at(i, "ql"))
                    act.activation(ql[d], ql[d], ACT.Exp).then_inc(act_[d].sem, 1)
                    for j in range(NB):
                        act.wait_ge(dve_[d].sem, dve_[d].at(i, f"kb{j}"))
                        kb = heads(KB[d][:, j * HALF:(j + 1) * HALF])[:, :, keys(d, j)]
                        act.activation(kb, kb, ACT.Exp).then_inc(act_[d].sem, 1)

            def transposed_gates(i):
                for d in range(2):
                    act.wait_ge(gate_pe[d].sem, gate_pe[d].at(i, "tg"))
                    act.copy(gT[d], bank(d, 2)[0:RANK, 0:P]).then_inc(gate_act[d].sem, 1)

            def transposed_scores(i):
                for d in range(2):
                    act.wait_ge(pe_[d].sem, pe_[d].at(i, "tA"))
                    act.copy(AT[d], bank(d, 1)).then_inc(act_[d].sem, 1)

            def log_gates(i):
                for d in range(2):
                    act.wait_ge(gate_dve[d].sem, gate_dve[d].at(i, "x"))
                    act.activation(la[d], x[d], ACT.Abs).then_inc(gate_act[d].sem, 1)
                for d in range(2):
                    act.wait_ge(gate_act[d].sem, gate_act[d].at(i, "abs"))
                    act.activation(la[d], la[d], ACT.Exp, scale=-1.0).then_inc(gate_act[d].sem, 1)
                for d in range(2):
                    act.wait_ge(gate_act[d].sem, gate_act[d].at(i, "exp"))
                    act.activation(la[d], la[d], ACT.Ln, bias=1.0).then_inc(gate_act[d].sem, 1)

            transposed_gates(0)
            log_gates(0)
            round_(0)
            transposed_gates(1)
            transposed_scores(0)
            log_gates(1)
            with act.Fori(1, NT - 1) as i:
                round_(i)
                transposed_gates(i + 1)
                transposed_scores(i)
                log_gates(i + 1)
            round_(NT - 1)
            transposed_scores(NT - 1)

        @block.tensor
        def _(pe):
            pe.wait_ge(loaded, 64)

            def transpose_gates(i):
                for d in range(2):
                    pe.wait_ge(gate_dve[d].sem, gate_dve[d].at(i, "g16"))
                    pe.transpose(bank(d, 2)[0:RANK, 0:P], g16[d], m.ident).then_inc(gate_pe[d].sem, 1)

            def gates(i):
                for d in range(2):
                    pe.wait_ge(gate_act[d].sem, gate_act[d].at(i, "gT"))
                    pe.matmul(bank(d, 3), gT[d], w2[d], start=True, stop=True).then_inc(gate_pe[d].sem, 1)

            def round_(i, last=False):
                tiles = tiles_of(pe, i)
                for d in range(2):
                    pe.wait_ge(pool_[d].sem, pool_[d].at(i, "qk"))
                    if not is_first(i):
                        pe.wait_ge(dve_[d].sem, dve_[d].at(i - 1, "S3"))
                    for n in range(2):
                        for h in range(NH):
                            tr = pe.transpose(bank(d, n)[:, h * P:(h + 1) * P],
                                              qk[d][:, n * HALF + h * P:n * HALF + (h + 1) * P], m.ident)
                        tr.then_inc(pe_[d].sem, 1)
                for d in range(2):
                    pe.wait_ge(gate_dve[d].sem, gate_dve[d].at(i, "la"))
                    for h in range(NH):
                        mm = pe.matmul(bank(d, 2)[:, h * P:(h + 1) * P], la[d][:, h * P:(h + 1) * P], cumulate[d],
                                       start=True, stop=True)
                    mm.then_inc(pe_[d].sem, 1)
                    pe.matmul(bank(d, 3), rest16[d], la[d], start=True, stop=True).then_inc(pe_[d].sem, 1)
                for d in range(2):
                    pe.wait_ge(act_[d].sem, act_[d].at(i, "kl"))
                if not last:
                    transpose_gates(i + 1)
                for d in range(2):
                    pe.wait_ge(dve_[d].sem, dve_[d].at(i, "keys3"))
                    for h in range(NH):
                        for j in range(NB):
                            mm = pe.matmul(bank(d, 0)[j * BL:(j + 1) * BL, h * P:(h + 1) * P],
                                           ql[d][:, h * P + j * BL:h * P + (j + 1) * BL],
                                           KB[d][:, j * HALF + h * P:j * HALF + (h + 1) * P], start=True, stop=True)
                    mm.then_inc(pe_[d].sem, 1)
                if not last:
                    gates(i + 1)
                for d in range(2):
                    pe.wait_ge(dve_[d].sem, dve_[d].at(i, "A"))
                    for h in range(NH):
                        tr = pe.transpose(bank(d, 1)[:, h * P:(h + 1) * P], A[d][:, h * P:(h + 1) * P], m.ident)
                    tr.then_inc(pe_[d].sem, 1)
                if not is_first(i):
                    pe.wait_ge(state_in, 32)
                for d, t in enumerate(tiles):
                    if not last:
                        pe.wait_ge(gate_dve[d].sem, gate_dve[d].at(i + 1, "x"))
                    pe.wait_ge(act_[d].sem, act_[d].at(i, "AT"))
                    for h in range(NH):
                        out = bank(d, 2 + h // 2)[:, (h % 2) * DV:(h % 2 + 1) * DV]
                        pe.matmul(out, AT[d][:, h * P:(h + 1) * P],
                                  m.proj[:, t, 2 * HALF + h * DV:2 * HALF + (h + 1) * DV], start=True, stop=False)
                        mm = pe.matmul(out, full[d][:, h * P:(h + 1) * P], S[d][:, h * DV:(h + 1) * DV],
                                       start=False, stop=True)
                    mm.then_inc(pe_[d].sem, 1)
                for d, t in enumerate(tiles):
                    for h in range(NH):
                        mm = pe.matmul(bank(d, h // 2)[:, (h % 2) * DV:(h % 2 + 1) * DV], kl[d][:, h * P:(h + 1) * P],
                                       m.proj[:, t, 2 * HALF + h * DV:2 * HALF + (h + 1) * DV], start=True, stop=True)
                    mm.then_inc(pe_[d].sem, 1)

            transpose_gates(0)
            gates(0)
            round_(0)
            with pe.Fori(1, NT - 1) as i:
                round_(i)
            round_(NT - 1, last=True)

        @block.vector
        def _(dve):
            dve.wait_ge(loaded, 64)

            def gates16(i, tiles):
                for d, t in enumerate(tiles):
                    dve.tensor_copy(g16[d], m.gates[:, t, RANK * d:RANK * (d + 1)]).then_inc(gate_dve[d].sem, 1)

            def gate_inputs(i):
                for d in range(2):
                    dve.wait_ge(gate_pe[d].sem, gate_pe[d].at(i, "gates"))
                    dve.tensor_tensor(x[d], bank(d, 3), bg[d], ALU.add).then_inc(gate_dve[d].sem, 1)

            def log_gates(i):
                for d in range(2):
                    dve.wait_ge(gate_act[d].sem, gate_act[d].at(i, "ln"))
                    dve.scalar_tensor_tensor(out=la[d], in0=x[d], scalar=0.0, in1=la[d], op0=ALU.min,
                                             op1=ALU.subtract).then_inc(gate_dve[d].sem, 1)

            def round_(i, last=False):
                tiles = tiles_of(dve, i)

                def after_act(d, step):
                    dve.wait_ge(act_[d].sem, act_[d].at(i, step))

                for d in range(2):
                    after_act(d, "bcS")
                    j0 = start_block(d)
                    dve.tensor_copy(blocks(ql[d])[:, :, j0, :], blocks(bcS[d])[:, :, j0, :]).then_inc(dve_[d].sem, 1)
                    others = slice(1, NB) if d == 0 else slice(0, NB - 1)
                    edge = blocks(bcS[d])[:, :, 0:NB - 1, BL - 1] if d == 0 else blocks(bcS[d])[:, :, 1:NB, 0]
                    dve.tensor_tensor(blocks(ql[d])[:, :, others, :], blocks(bcS[d])[:, :, others, :],
                                      edge.unsqueeze(3).to_broadcast([P, NH, NB - 1, BL]), ALU.subtract)\
                        .then_inc(dve_[d].sem, 1)
                    for j in range(NB):
                        kb = heads(KB[d][:, j * HALF:(j + 1) * HALF])[:, :, keys(d, j)]
                        src = heads(bcS[d])[:, :, keys(d, j)]
                        if before(d, j) is None:
                            ins = dve.tensor_scalar(kb, src, -1.0, None, ALU.mult)
                        else:
                            edge = heads(bcS[d])[:, :, before(d, j):before(d, j) + 1]
                            ins = dve.tensor_tensor(kb, edge.to_broadcast([P, NH, src.shape[2]]), src, ALU.subtract)
                        ins.then_inc(dve_[d].sem, 1)
                if not last:
                    gates16(i + 1, tiles_of(dve, i, 1))
                for d, t in enumerate(tiles):
                    after_act(d, "full")
                    dve.tensor_copy(decay[d], heads(full[d])[:, :, final[d]]).then_inc(dve_[d].sem, 1)
                    after_act(d, "ql")
                    dve.tensor_tensor(ql[d], ql[d], qT[d], ALU.mult).then_inc(dve_[d].sem, 1)
                    dve.wait_ge(dve_[d].sem, dve_[d].at(i, "decay"))
                    dve.tensor_tensor(full[d], full[d], qT[d], ALU.mult).then_inc(dve_[d].sem, 1)
                    dve.tensor_tensor(kl[d], kl[d], m.proj[:, t, HALF:2 * HALF], ALU.mult).then_inc(dve_[d].sem, 1)
                    for j in range(NB):
                        after_act(d, f"kb{j}")
                        kb = heads(KB[d][:, j * HALF:(j + 1) * HALF])[:, :, keys(d, j)]
                        dve.tensor_tensor(kb, kb, heads(kT[d])[:, :, keys(d, j)], ALU.mult).then_inc(dve_[d].sem, 1)
                for d in range(2):
                    dve.wait_ge(pe_[d].sem, pe_[d].at(i, "A"))
                    dve.tensor_tensor(heads(A[d]), heads(bank(d, 0)), causal[d].unsqueeze(1).to_broadcast([P, NH, P]),
                                      ALU.mult).then_inc(dve_[d].sem, 1)
                if not last:
                    gate_inputs(i + 1)
                for d, t in enumerate(tiles):
                    if d == 1 and not last:
                        log_gates(i + 1)
                    dve.wait_ge(pe_[d].sem, pe_[d].at(i, "o"))
                    if is_first(i) and d == 1:
                        dve.wait_ge(dve_[0].sem, dve_[0].at(i, "o"))
                    out = m.H[:, t, :]
                    dve.tensor_tensor(out, out, m.ps[:, 4 * d + 2:4 * d + 4, :].rearrange("p b n -> p (b n)"),
                                      ALU.add).then_inc(dve_[d].sem, 1)
                if not is_first(i):
                    dve.wait_ge(state_in, 32)
                for d in range(2):
                    dve.wait_ge(pe_[d].sem, pe_[d].at(i, "dS"))
                    for h in range(NH):
                        state = S[d][:, h * DV:(h + 1) * DV]
                        dve.scalar_tensor_tensor(out=state, in0=state, scalar=decay[d][:, h:h + 1],
                                                 in1=bank(d, h // 2)[:, (h % 2) * DV:(h % 2 + 1) * DV],
                                                 op0=ALU.mult, op1=ALU.add).then_inc(dve_[d].sem, 1)

            gates16(0, (0, 0))
            gate_inputs(0)
            log_gates(0)
            dve.wait_ge(cleared, 5)
            round_(0)
            with dve.Fori(1, NT - 1) as i:
                round_(i)
            round_(NT - 1, last=True)


ROUTE = ("mx0 mx1 ix0 ix1 cut0 cut1 mxb0 mxb1 ixb0 ixb1 idxf0 idxf cand mxc ixc cutc mxd ixd "
         "row col rc hot picked pair expert neg rsum gate")


def peer(nc, m, a, layer):
    RB = RING
    TURN = 2 * NT
    TURNS = EH // 2
    LEAD = 2
    LAST_PE = 6
    w_q = a["peer_w_q"][layer].rearrange("(k p) n -> p k n", p=P)
    u, v = (a[name].rearrange("l e n -> (l e) n") for name in ("peer_u", "peer_v"))
    at = [0]

    def part(n, buf=m.wrk):
        at[0] += n
        return buf[:, at[0] - n:at[0]]

    flat = lambda x: x.rearrange("p a n -> p (a n)")
    wq = [x.rearrange("p (k n) -> p k n", k=KD) for x in (flat(m.lnw[:]), part(2 * KD * P))]
    sk = part(2 * EH * NKEYS).rearrange("p (g n) -> p g n", g=EH)
    xm = [part(D) for _ in range(NT)]
    acc = [part(D) for _ in range(NT)]
    assert at[0] <= m.wrk.shape[1]
    ring = [m.big[:, r * D:(r + 1) * D] for r in range(RB - 4)] + [m.mod[:, n, c, :] for n in range(2) for c in range(2)]
    xT = [m.big[:, (RB - 4 + t) * D:(RB - 3 + t) * D].rearrange("p (k n) -> p k n", k=KD) for t in range(NT - 1)] + [m.yT[:]]
    diag = [x[:, r * P:(r + 1) * P] for x in (m.y, m.diag) for r in range(KD)]
    at[0] = 0
    small = lambda n: part(n, m.qk)
    expert = small(NT * EH * TOPK).bitcast(U32)
    gates = m.route_gate[:]
    stage = [small(TOPK).bitcast(U32) for _ in range(2)]
    qh = [m.qhT[:, 0], m.qhT[:, 1]]
    s, s2 = small(2 * NKEYS), small(2 * NKEYS)
    top = small(2 * TOPK)
    idx = small(2 * TOPK).bitcast(U32)
    idxf = small(2 * TOPK)
    cand, cand2 = small(TOPK * TOPK), m.scr[:, 0:TOPK * TOPK]
    best, pos = small(TOPK), small(TOPK).bitcast(U32)
    rc, rcf, pair = small(2 * TOPK).bitcast(U32), small(2 * TOPK), small(2 * TOPK)
    ge, neg, rsum = small(TOPK), small(1), small(1)
    act_u, tanh, wv, t1 = ([small(TOPK) for _ in range(2)] for _ in range(4))
    assert at[0] <= m.qk.shape[1]
    hot = m.hot[:]
    three = lambda ap: ap.rearrange("p (a b) -> p a b", b=TOPK)
    four = lambda ap: ap.rearrange("p (c a b) -> p c a b", c=2, b=TOPK)

    with Stage(nc, f"peer{layer}") as st:
        route = Order(st.sem("route"), ROUTE)
        route_act = Order(st.sem("route_act"), "qh scores exp")
        route_pe = Order(st.sem("route_pe"), "qh scores")
        prep = Order(st.sem("prep"), "scaled shifted")
        gelu = Order(st.sem("gelu"), "sq cubic arg half weight")
        gelu_act = Order(st.sem("gelu_act"), "tanh")
        fin = Order(st.sem("fin"), "scaled added " + NORM + " done")
        fin_act = Order(st.sem("fin_act"), "sqrt")
        stored = st.sem("stored")
        w_full = [st.sem("w_full0"), st.sem("w_full1")]
        landed = [st.sem(f"landed{r}") for r in range(RB)]
        rows_in, sk_in, used_u, used_v, diagonals, summed, staged, xT_done, xT_copied, passed, gather_passed, own_v = (
            st.sem(n) for n in ("rows_in", "sk_in", "used_u", "used_v", "diagonals", "summed", "staged", "xT_done",
                                "xT_copied", "passed", "gather_passed", "own_v"))
        block = st.block()
        v_bank = lambda b: 6 * b

        @block.sync
        def _(sp):
            def load_heads(n):
                for e in range(2):
                    if not is_first(n):
                        sp.wait_ge(route_pe.sem, route_pe.at(((n - 1) * 2 + e) * NT + NT - 1, "qh"))
                    sp.dma_start(wq[e], w_q[:, :, bass.ds((n * 2 + e) * 2 * P, 2 * P)]).then_inc(w_full[e], 16)

            load_heads(0)
            sp.dma_start(sk, a["subkeysT"][layer]).then_inc(sk_in, 16)
            with sp.Fori(1, TURNS) as n:
                load_heads(n)
            sp.wait_ge(route_pe.sem, route_pe.at((EH - 1) * NT - 1, "qh"))
            load_rows(sp, m, a, layer, 3, (2,), "ffn", rows_in)
            sp.wait_ge(rows_in, 16 * 4)
            if layer == LAYERS - 1:
                for t in range(NT):
                    y = a["y_prompt"][0] if t == 0 else a["y_sample"][0, (t - 1) * P:t * P, :]
                    sp.wait_ge(fin.sem, fin.at(t, "done"))
                    sp.dma_start(y, m.X[:, t, :]).then_inc(stored, 16)
                sp.wait_ge(stored, 16 * NT)

        @block.tensor
        def _(pe):
            def transpose(t):
                pe.wait_ge(prep.sem, prep.at(t, "shifted"))
                if t >= 2:
                    pe.wait_ge(xT_copied, t - 1)
                for k in range(KD):
                    tr = pe.transpose(m.ps[:, v_bank(t % 2) + k // 4, (k % 4) * P:(k % 4 + 1) * P],
                                      xm[t][:, k * P:(k + 1) * P], m.ident)
                tr.then_inc(xT_done, 1)

            def head(n, q):
                R, t, b, e = n * TURN + q, q % NT, q % 2, q // NT
                if t == 0:
                    pe.wait_ge(w_full[e % 2], (n + e // 2 + 1) * 16)
                if is_first(n) and q < LEAD:
                    pe.wait_ge(xT_copied, t + 1)
                else:
                    pe.wait_ge(route_act.sem, route_act.at(R - 2, "scores"))
                for p in range(2):
                    for k in range(KD):
                        mm = pe.matmul(m.ps[:, 2 + b, p * P:(p + 1) * P], wq[e % 2][:, k, p * P:(p + 1) * P], xT[t][:, k, :],
                                       start=k == 0, stop=k == KD - 1)
                mm.then_inc(route_pe.sem, 1)
                pe.wait_ge(route_act.sem, route_act.at(R, "qh"))
                if is_first(n) and q == 0:
                    pe.wait_ge(sk_in, 16)
                for p in range(2):
                    mm = pe.matmul(m.ps[:, 4 + b, p * P:(p + 1) * P], qh[b][:, p * P:(p + 1) * P],
                                   sk[:, n * 2 + e, p * NKEYS:(p + 1) * NKEYS], start=True, stop=True)
                mm.then_inc(route_pe.sem, 1)

            def sum_v(n, q, rows=TOPK):
                G, b = n * TURN + q, q % 2
                pe.wait_ge(summed, G + NT - 1)
                for r in range(rows):
                    pe.wait_ge(landed[r], (G * 2 + 2) * 16)
                    pe.wait_ge(diagonals, G * TOPK + r + 1)
                    for h in range(2):
                        mm = pe.matmul(m.ps[:, v_bank(b) + h, :], diag[r], ring[r][:, h * HALF:(h + 1) * HALF],
                                       start=r == 0, stop=r == rows - 1)
                    mm.then_inc(used_v, 1)

            pe.sem_inc(used_v, RB)
            for q in range(LEAD):
                transpose(q)
                head(0, q)
            for t in range(LEAD, NT):
                transpose(t)
            pe.wait_ge(xT_copied, NT)
            with pe.Fori(0, TURNS - 1) as n:
                for q in range(TURN):
                    head(n, q + LEAD)
                    sum_v(n, q)
            for q in range(TURN):
                if q + LEAD < TURN:
                    head(TURNS - 1, q + LEAD)
                sum_v(TURNS - 1, q, TOPK if q < TURN - 1 else LAST_PE)

        @block.scalar
        def _(act):
            def copy_xT(t):
                act.wait_ge(xT_done, t + 1)
                b = v_bank(t % 2)
                act.copy(flat(xT[t]), flat(m.ps[:, b:b + 2, :])).then_inc(xT_copied, 1)

            def scores(R, b, first):
                act.wait_ge(route_pe.sem, route_pe.at(R, "qh"))
                act.copy(qh[b], m.ps[:, 2 + b, 0:2 * P]).then_inc(route_act.sem, 1)
                act.wait_ge(route_pe.sem, route_pe.at(R, "scores"))
                if not first:
                    act.wait_ge(route.sem, route.at(R - 1, "cut1"))
                act.copy(s, m.ps[:, 4 + b, 0:2 * NKEYS]).then_inc(route_act.sem, 1)

            def exp(R):
                act.wait_ge(route.sem, route.at(R, "neg"))
                act.activation(ge, best, ACT.Exp, bias=neg, accum_out=rsum).then_inc(route_act.sem, 1)

            def tanh_(G, b):
                act.wait_ge(gelu.sem, gelu.at(G, "arg"))
                act.activation(tanh[b], t1[b], ACT.Tanh, scale=TANH_SCALE).then_inc(gelu_act.sem, 1)

            def diagonal(G, b):
                act.wait_ge(gelu.sem, gelu.at(G, "weight"))
                act.wait_ge(used_v, G * TOPK + RB)
                for r in range(TOPK):
                    act.activation(diag[r], m.ident, ACT.Copy, scale=wv[b][:, r:r + 1]).then_inc(diagonals, 1)

            def group(n, q, routed):
                G, b = n * TURN + q, q % 2
                if routed:
                    scores(G + LEAD, b, False)
                tanh_(G, b)
                diagonal(G, b)
                if routed:
                    exp(G + LEAD)

            for q in range(LEAD):
                copy_xT(q)
                scores(q, q, q == 0)
                if q == 0:
                    exp(q)
            for t in range(LEAD, NT):
                copy_xT(t)
            exp(LEAD - 1)
            with act.Fori(0, TURNS - 1) as n:
                for q in range(TURN):
                    group(n, q, True)
            for q in range(TURN):
                group(TURNS - 1, q, q + LEAD < TURN)
                if q >= NT:
                    layer_norm_sqrt(act, m, fin, fin_act, q - NT)

        @block.gpsimd
        def _(pool):
            for t in range(NT):
                pool.memset(acc[t], 0.0).then_inc(summed, 1)
            with pool.Fori(0, EH * NT // 2) as i:
                for b in range(2):
                    G = i * 2 + b
                    pool.wait_ge(used_v, G * TOPK + 4)
                    pool.wait_ge(route.sem, route.at(G, "expert"))
                    pool.tensor_copy(stage[b], expert[:, bass.ds(G * TOPK, TOPK)]).then_inc(staged, 1)
                    pool.wait_ge(staged, G + 1)
                    pool.sem_inc(gather_passed, 1)
                    for table, used, free in ((u, used_v, RB), (v, used_u, 0)):
                        for r in range(TOPK):
                            if r % 4 == 0:
                                pool.wait_ge(used, G * TOPK + r + 4 + free - (TOPK if table is u else 0))
                                pool.sem_inc(gather_passed, 1)
                            if table is u and r == RB - 4:
                                pool.wait_ge(prep.sem, prep.at(NT - 1, "shifted"))
                            pool.indirect_dma_start(ring[r], None, table,
                                                    bass.IndirectOffsetOnAxis(ap=stage[b][:, r:r + 1], axis=0))\
                                .then_inc(landed[r], 16)

        @block.vector
        def _(dve):
            def prepare(t):
                c = min(t, 1)
                dve.scalar_tensor_tensor(out=xm[t], in0=m.mod[:, 1, c, :], scalar=1.0, in1=m.X[:, t, :], op0=ALU.add,
                                         op1=ALU.mult).then_inc(prep.sem, 1)
                dve.wait_ge(prep.sem, prep.at(t, "scaled"))
                dve.tensor_tensor(xm[t], xm[t], m.mod[:, 0, c, :], ALU.add).then_inc(prep.sem, 1)

            def route_head(R):
                def own(step):
                    dve.wait_ge(route.sem, route.at(R, step))

                half = lambda x, p: x[:, p * TOPK:(p + 1) * TOPK]
                key = lambda x, p: x[:, p * NKEYS:(p + 1) * NKEYS]
                dve.wait_ge(route_act.sem, route_act.at(R, "scores"))
                dve.sem_inc(passed, 1)
                for p in range(2):
                    dve.max(half(top, p)[:, 0:8], key(s, p)).then_inc(route.sem, 1)
                for p in range(2):
                    dve.wait_ge(route.sem, route.at(R, f"mx{p}"))
                    dve.sem_inc(passed, 1)
                    dve.max_index(half(idx, p)[:, 0:8], half(top, p)[:, 0:8], key(s, p)).then_inc(route.sem, 1)
                for p in range(2):
                    dve.match_replace(key(s2, p), half(top, p)[:, 0:8], key(s, p), NEG).then_inc(route.sem, 1)
                for p in range(2):
                    dve.wait_ge(route.sem, route.at(R, f"cut{p}"))
                    dve.sem_inc(passed, 1)
                    dve.max(half(top, p)[:, 8:16], key(s2, p)).then_inc(route.sem, 1)
                for p in range(2):
                    dve.wait_ge(route.sem, route.at(R, f"mxb{p}"))
                    dve.sem_inc(passed, 1)
                    dve.max_index(half(idx, p)[:, 8:16], half(top, p)[:, 8:16], key(s2, p)).then_inc(route.sem, 1)
                own("ixb1")
                dve.tensor_scalar(half(idxf, 0), half(idx, 0), float(layer * NKEYS), None, ALU.add).then_inc(route.sem, 1)
                dve.tensor_copy(half(idxf, 1), half(idx, 1)).then_inc(route.sem, 1)
                dve.tensor_tensor(three(cand), half(top, 0).unsqueeze(2).to_broadcast([P, TOPK, TOPK]),
                                  half(top, 1).unsqueeze(1).to_broadcast([P, TOPK, TOPK]), ALU.add).then_inc(route.sem, 1)
                own("cand")
                dve.sem_inc(passed, 1)
                dve.max(best[:, 0:8], cand).then_inc(route.sem, 1)
                own("mxc")
                dve.sem_inc(passed, 1)
                dve.max_index(pos[:, 0:8], best[:, 0:8], cand).then_inc(route.sem, 1)
                dve.match_replace(cand2, best[:, 0:8], cand, NEG).then_inc(route.sem, 1)
                own("cutc")
                dve.sem_inc(passed, 1)
                dve.max(best[:, 8:16], cand2).then_inc(route.sem, 1)
                own("mxd")
                dve.sem_inc(passed, 1)
                dve.max_index(pos[:, 8:16], best[:, 8:16], cand2).then_inc(route.sem, 1)
                own("ixd")
                dve.tensor_scalar(half(rc, 0), pos, 4, None, ALU.logical_shift_right).then_inc(route.sem, 1)
                dve.tensor_scalar(half(rc, 1), pos, TOPK - 1, None, ALU.bitwise_and).then_inc(route.sem, 1)
                own("col")
                dve.tensor_copy(rcf, rc).then_inc(route.sem, 1)
                own("rc")
                dve.tensor_tensor(four(hot), three(rcf).unsqueeze(3).to_broadcast([P, 2, TOPK, TOPK]),
                                  m.iota.unsqueeze(1).unsqueeze(1).to_broadcast([P, 2, TOPK, TOPK]), ALU.is_equal)\
                    .then_inc(route.sem, 1)
                own("hot")
                dve.tensor_tensor(four(hot), four(hot), three(idxf).unsqueeze(2).to_broadcast([P, 2, TOPK, TOPK]),
                                  ALU.mult).then_inc(route.sem, 1)
                own("picked")
                dve.tensor_reduce(three(pair), four(hot), AX.X, ALU.add).then_inc(route.sem, 1)
                own("pair")
                dve.scalar_tensor_tensor(out=expert[:, bass.ds(R * TOPK, TOPK)], in0=half(pair, 0), scalar=float(NKEYS),
                                         in1=half(pair, 1), op0=ALU.mult, op1=ALU.add).then_inc(route.sem, 1)
                dve.tensor_scalar(neg, best[:, 0:1], -1.0, None, ALU.mult).then_inc(route.sem, 1)
                dve.wait_ge(route_act.sem, route_act.at(R, "exp"))
                dve.reciprocal(rsum, rsum).then_inc(route.sem, 1)
                own("rsum")
                dve.tensor_scalar(gates[:, bass.ds(R * TOPK, TOPK)], ge, rsum, 0.5, ALU.mult, ALU.mult)\
                    .then_inc(route.sem, 1)

            def dots(G, t, b):
                for r in range(TOPK):
                    dve.wait_ge(landed[r], (G * 2 + 1) * 16)
                    dve.scalar_tensor_tensor(out=ring[r], in0=ring[r], scalar=1.0, in1=xm[t], op0=ALU.mult,
                                             op1=ALU.mult, accum_out=act_u[b][:, r:r + 1]).then_inc(used_u, 1)

            def weights(G, b):
                own = lambda step: dve.wait_ge(gelu.sem, gelu.at(G, step))
                dve.wait_ge(used_u, (G + 1) * TOPK)
                dve.tensor_tensor(t1[b], act_u[b], act_u[b], ALU.mult).then_inc(gelu.sem, 1)
                own("sq")
                dve.tensor_scalar(t1[b], t1[b], 0.044715, 1.0, ALU.mult, ALU.add).then_inc(gelu.sem, 1)
                own("cubic")
                dve.tensor_tensor(t1[b], t1[b], act_u[b], ALU.mult).then_inc(gelu.sem, 1)
                dve.wait_ge(gelu_act.sem, gelu_act.at(G, "tanh"))
                dve.scalar_tensor_tensor(out=wv[b], in0=tanh[b], scalar=1.0, in1=act_u[b], op0=ALU.add, op1=ALU.mult)\
                    .then_inc(gelu.sem, 1)
                own("half")
                dve.tensor_tensor(wv[b], wv[b], gates[:, bass.ds(G * TOPK, TOPK)], ALU.mult).then_inc(gelu.sem, 1)

            def group(n, q, routed, last):
                G, t, b = n * TURN + q, q % NT, q % 2
                own = lambda step: dve.wait_ge(gelu.sem, gelu.at(G, step))
                weights(G, b)
                if routed:
                    route_head(G + LEAD)
                if last:
                    own("weight")
                    dve.wait_ge(summed, G + 1)
                    for n, r in enumerate(range(LAST_PE, TOPK)):
                        dve.wait_ge(landed[r], (G * 2 + 2) * 16)
                        if n > 0:
                            dve.wait_ge(own_v, n)
                        dve.scalar_tensor_tensor(out=acc[t], in0=ring[r], scalar=wv[b][:, r:r + 1], in1=acc[t],
                                                 op0=ALU.mult, op1=ALU.add).then_inc(own_v, 1)
                    dve.wait_ge(own_v, TOPK - LAST_PE)
                else:
                    dots(G + 1, (q + 1) % NT, 1 - b)
                dve.wait_ge(used_v, G * TOPK + (LAST_PE if last else TOPK) + RB)
                dve.wait_ge(summed, G + 1)
                dve.tensor_tensor(acc[t], acc[t], flat(m.ps[:, v_bank(b):v_bank(b) + 2, :]), ALU.add).then_inc(summed, 1)

            def finish(t):
                own = lambda step: dve.wait_ge(fin.sem, fin.at(t, step))
                z, c = acc[t], min(t, 1)
                dve.wait_ge(summed, NT + (TURNS - 1) * TURN + NT + t + 1)
                if t == 0:
                    dve.wait_ge(rows_in, 16 * 4)
                else:
                    dve.wait_ge(fin.sem, fin.at(t - 1, "done"))
                dve.tensor_tensor(z, z, m.mod[:, 2, c, :], ALU.mult).then_inc(fin.sem, 1)
                own("scaled")
                dve.scalar_tensor_tensor(out=z, in0=m.X[:, t, :], scalar=ALPHA, in1=z, op0=ALU.mult,
                                         op1=ALU.add).then_inc(fin.sem, 1)
                layer_norm(nc, dve, m, fin, fin_act, t, z, m.X[:, t, :], "added", passed)

            prepare(0)
            prepare(1)
            route_head(0)
            for t in range(LEAD, NT):
                prepare(t)
            route_head(1)
            dots(0, 0, 0)
            with dve.Fori(0, TURNS - 1) as n:
                for q in range(TURN):
                    group(n, q, True, False)
            for q in range(TURN):
                group(TURNS - 1, q, q + LEAD < TURN, q == TURN - 1)
                if q >= NT:
                    finish(q - NT)


def trunk(nc, a, const_cols, where):
    a = dict(a, rows=nc.dram_tensor("modulation_rows", (LAYERS, 2, CHUNKS * D), F32).ap())
    with ExitStack() as ctx:
        m = allocate(nc, ctx, const_cols)
        view_constants(m, where)
        for layer in range(LAYERS):
            if layer == 0:
                modulation_rows(nc, m, a, layer)
            project(nc, m, a, layer)
            (mlstm_scan, gla_scan)[layer](nc, m, a)
            mixer_output(nc, m, a, layer)
            peer(nc, m, a, layer)


_PLAIN = ["x_prompt", "x_sample", "state_mlstm_C", "state_mlstm_n", "state_mlstm_m", "state_gla_S", "ada_w", "ada_b",
          "ln_mix_g", "ln_mix_b", "ln_ffn_g", "ln_ffn_b", "mlstm_w_in", "mlstm_b_gate", "mlstm_norm_w", "mlstm_w_out",
          "gla_w_in", "gla_w_gate2", "gla_b_gate2", "gla_norm_w", "gla_w_out", "peer_w_q", "peer_u", "peer_v"]
_OUTS = {"y_prompt": (1, SEQ, D), "y_sample": (1, DEC_SEQ, D), "new_C": (1, 2, NH, DK, DV), "new_n": (1, 2, NH, DK),
         "new_m": (1, 2, NH), "new_S": (1, 2, NH, DK, DV)}


def kernel(**inputs):
    import numpy as _np
    import concourse.bacc as _bacc
    from concourse import mybir as _mybir
    from concourse.bass_utils import run_bass_kernel_spmd as _run

    host = {name: _np.asarray(inputs[name]) for name in _PLAIN}
    cond = _np.stack([_np.asarray(inputs["c_ctx"]), _np.asarray(inputs["c"])[0]], -1)
    host["c2"] = cond.reshape(KD, P, 2).transpose(1, 0, 2).reshape(P, 2 * KD)
    host["subkeysT"] = _np.asarray(inputs["peer_subkeys"]).transpose(0, 4, 1, 2, 3).reshape(LAYERS, P, EH, 2 * NKEYS)
    host["cst"], where = constants()
    nc = _bacc.Bacc("TRN2", target_bir_lowering=False, num_devices=1)
    arrays, a = {}, {}
    for name, array in host.items():
        array = _np.ascontiguousarray(array)
        arrays["in_" + name] = array
        a[name] = nc.dram_tensor("in_" + name, array.shape, _mybir.dt.from_np(array.dtype), kind="ExternalInput").ap()
    for name, shape in _OUTS.items():
        a[name] = nc.dram_tensor("out_" + name, shape, F32, kind="ExternalOutput").ap()
    trunk(nc, a, host["cst"].shape[1], where)
    r = _run(nc, [arrays], core_ids=[0])
    return tuple(r.results[0]["out_" + name] for name in _OUTS) + (None,) * 4
```
